# Optimizing a Trainium2 kernel written in Bass

```python
import jax, jax.numpy as jnp
from jax import lax
import numpy as np

D_MODEL = 1024
BATCH = 1
SEQ = 256
DEPTH = 1

HEAD_DIM = 64
N_Q_HEADS = 8
N_KV_HEADS = 2
Q_PER_KV = N_Q_HEADS // N_KV_HEADS
ATTN_WIDTH = N_Q_HEADS * HEAD_DIM
KV_WIDTH = N_KV_HEADS * HEAD_DIM
WINDOW = 128
ATT_BLOCK = 128
CHUNK = 128
N_SG_GROUPS = 8
SG_GROUP_DIM = 64
SG_WIDTH = N_SG_GROUPS * SG_GROUP_DIM
SPLIT_SIZES = (ATTN_WIDTH, KV_WIDTH, KV_WIDTH, SG_WIDTH, SG_WIDTH, D_MODEL, D_MODEL)
IN_WIDTH = sum(SPLIT_SIZES)
SPLIT_POINTS = tuple(int(v) for v in np.cumsum(SPLIT_SIZES)[:-1])
N_EXPERTS = 32
TOP_K = 4
D_EXPERT = D_MODEL
SWIGLU_LIMIT = 7.0
SWIGLU_ALPHA = 1.702
MOE_BLOCK = 256
NORM_EPS = 1e-6

kernel_name = 'hybrid_gmlp_swa_sink_moe_block'

def rmsnorm(x, g):
    xf = x.astype(jnp.float32)
    xf = xf * lax.rsqrt(jnp.mean(xf * xf, axis=-1, keepdims=True) + NORM_EPS)
    return (xf * g.astype(jnp.float32)).astype(x.dtype)

def layernorm(x, g, b):
    xf = x.astype(jnp.float32)
    mu = jnp.mean(xf, axis=-1, keepdims=True)
    var = jnp.mean(jnp.square(xf - mu), axis=-1, keepdims=True)
    y = (xf - mu) * lax.rsqrt(var + NORM_EPS) * g.astype(jnp.float32) + b.astype(jnp.float32)
    return y.astype(x.dtype)

def alibi_slopes(n_heads):
    return jnp.asarray(2.0 ** (-8.0 * np.arange(1, n_heads + 1) / n_heads), dtype=jnp.float32)

def sliding_window_attention(q, k, v, sinks):
    B, S, _ = q.shape
    nb = S // ATT_BLOCK
    q = q.reshape(B, nb, ATT_BLOCK, N_KV_HEADS, Q_PER_KV, HEAD_DIM)
    k = k.reshape(B, nb, ATT_BLOCK, N_KV_HEADS, HEAD_DIM)
    v = v.reshape(B, nb, ATT_BLOCK, N_KV_HEADS, HEAD_DIM)

    def with_prev(t):
        prev = jnp.pad(t[:, :-1], ((0, 0), (1, 0), (0, 0), (0, 0), (0, 0)))
        return jnp.concatenate([prev, t], axis=2)

    kb, vb = with_prev(k), with_prev(v)
    scores = jnp.einsum('bnqhgd,bnkhd->bnhgqk', q, kb,
                        preferred_element_type=jnp.float32) * (HEAD_DIM ** -0.5)
    qi = jnp.arange(ATT_BLOCK)[:, None]
    kj = jnp.arange(2 * ATT_BLOCK)[None, :]
    dist = qi + ATT_BLOCK - kj
    in_win = (dist >= 0) & (dist < WINDOW)
    blk = jnp.arange(nb)[:, None, None]
    mask = in_win[None] & ((blk > 0) | (kj[None] >= ATT_BLOCK))
    slopes = alibi_slopes(N_Q_HEADS).reshape(N_KV_HEADS, Q_PER_KV)
    logits = scores - slopes[:, :, None, None] * dist.astype(jnp.float32)
    logits = jnp.where(mask[None, :, None, None], logits, -jnp.inf)
    sink = sinks.astype(jnp.float32).reshape(N_KV_HEADS, Q_PER_KV)[None, None, :, :, None, None]
    m = jnp.maximum(jnp.max(logits, axis=-1, keepdims=True), sink)
    p = jnp.exp(logits - m)
    probs = p / (jnp.sum(p, axis=-1, keepdims=True) + jnp.exp(sink - m))
    out = jnp.einsum('bnhgqk,bnkhd->bnqhgd', probs.astype(v.dtype), vb)
    return out.reshape(B, S, ATTN_WIDTH)

def chunked_spatial_gating(u, v, ln_g, ln_b, w_s, b_s):
    B, S, _ = u.shape
    nc = S // CHUNK
    vn = layernorm(v, ln_g, ln_b).reshape(B, nc, CHUNK, N_SG_GROUPS, SG_GROUP_DIM)
    causal = jnp.tril(jnp.ones((CHUNK, CHUNK), dtype=bool))
    w = jnp.where(causal[None], w_s, 0.0).astype(vn.dtype)
    mixed = jnp.einsum('gts,bcsgd->bctgd', w, vn) + b_s.T.astype(vn.dtype)[None, None, :, :, None]
    return u * mixed.reshape(B, S, SG_WIDTH)

def moe_ffn(h, w_router, b_router, w1, b1, w2, b2):
    B, S, D = h.shape
    T = B * S
    xt = h.reshape(T, D)
    logits = (xt @ w_router).astype(jnp.float32) + b_router.astype(jnp.float32)
    top_vals, top_idx = lax.top_k(logits, TOP_K)
    gates = jax.nn.softmax(top_vals, axis=-1)
    A = T * TOP_K
    flat_e = top_idx.reshape(A)
    flat_tok = jnp.arange(A, dtype=jnp.int32) // TOP_K
    flat_w = gates.reshape(A)
    order = jnp.argsort(flat_e, stable=True)
    se, stok, sw = flat_e[order], flat_tok[order], flat_w[order]
    counts = jnp.bincount(flat_e, length=N_EXPERTS)
    padded = (counts + MOE_BLOCK - 1) // MOE_BLOCK * MOE_BLOCK
    starts = jnp.cumsum(counts) - counts
    pends = jnp.cumsum(padded)
    pstarts = pends - padded
    slot = pstarts[se] + (jnp.arange(A, dtype=jnp.int32) - starts[se])
    n_blocks = -(-A // MOE_BLOCK) + N_EXPERTS
    P = n_blocks * MOE_BLOCK
    slot_tok = jnp.full((P,), T, dtype=jnp.int32).at[slot].set(stok)
    slot_w = jnp.zeros((P,), dtype=jnp.float32).at[slot].set(sw)
    block_start = jnp.arange(n_blocks, dtype=pends.dtype) * MOE_BLOCK
    block_e = jnp.minimum(jnp.searchsorted(pends, block_start, side='right'), N_EXPERTS - 1)
    x_pad = jnp.concatenate([xt, jnp.zeros((1, D), xt.dtype)], axis=0)
    xs = x_pad[slot_tok].reshape(n_blocks, MOE_BLOCK, D)

    def expert_block(args):
        xb, e = args
        hb = xb @ w1[e] + b1[e]
        g, lin = hb[:, :D_EXPERT], hb[:, D_EXPERT:]
        g = jnp.minimum(g, SWIGLU_LIMIT)
        lin = jnp.clip(lin, -SWIGLU_LIMIT, SWIGLU_LIMIT)
        act = g * jax.nn.sigmoid(SWIGLU_ALPHA * g) * (lin + 1.0)
        return act @ w2[e] + b2[e]

    ys = lax.map(expert_block, (xs, block_e)).reshape(P, D)
    ys = ys * slot_w[:, None].astype(ys.dtype)
    out = jax.ops.segment_sum(ys, slot_tok, num_segments=T + 1)[:T]
    return out.reshape(B, S, D)

def setup_inputs(seed: int = 0) -> dict:
    key = jax.random.key(seed)
    ks = jax.random.split(key, 28)
    L, D, E, I = DEPTH, D_MODEL, N_EXPERTS, D_EXPERT
    nrm = lambda k, shape, s: jax.random.normal(k, shape, jnp.float32) * s
    gain = lambda k, shape: 1.0 + 0.05 * jax.random.normal(k, shape, jnp.float32)
    return {
        'x': nrm(ks[0], (BATCH, SEQ, D), 1.0),
        'c': nrm(ks[1], (BATCH, D), 1.0),
        'w_mod': nrm(ks[2], (L, D, 6 * D), D ** -0.5),
        'b_mod': nrm(ks[3], (L, 6 * D), 0.02),
        'g_pre_mix': gain(ks[4], (L, D)),
        'g_post_mix': gain(ks[5], (L, D)),
        'w_in': nrm(ks[6], (L, D, IN_WIDTH), D ** -0.5),
        'b_in': nrm(ks[7], (L, IN_WIDTH), 0.02),
        'attn_sinks': nrm(ks[8], (L, N_Q_HEADS), 0.5),
        'sg_ln_g': gain(ks[9], (L, SG_WIDTH)),
        'sg_ln_b': nrm(ks[10], (L, SG_WIDTH), 0.02),
        'sg_w': nrm(ks[11], (L, N_SG_GROUPS, CHUNK, CHUNK), CHUNK ** -0.5),
        'sg_b': gain(ks[12], (L, N_SG_GROUPS, CHUNK)),
        'w_br_attn': nrm(ks[13], (L, ATTN_WIDTH, D), ATTN_WIDTH ** -0.5),
        'w_br_sg': nrm(ks[14], (L, SG_WIDTH, D), SG_WIDTH ** -0.5),
        'w_out': nrm(ks[15], (L, D, D), D ** -0.5),
        'b_out': nrm(ks[16], (L, D), 0.02),
        'g_pre_ffn': gain(ks[17], (L, D)),
        'g_post_ffn': gain(ks[18], (L, D)),
        'w_router': nrm(ks[19], (L, D, E), D ** -0.5),
        'b_router': nrm(ks[20], (L, E), 0.01),
        'w_mlp1': nrm(ks[21], (L, E, D, 2 * I), D ** -0.5),
        'b_mlp1': nrm(ks[22], (L, E, 2 * I), 0.02),
        'w_mlp2': nrm(ks[23], (L, E, I, D), I ** -0.5),
        'b_mlp2': nrm(ks[24], (L, E, D), 0.02),
    }

def reference(x, c, w_mod, b_mod, g_pre_mix, g_post_mix, w_in, b_in, attn_sinks,
              sg_ln_g, sg_ln_b, sg_w, sg_b, w_br_attn, w_br_sg, w_out, b_out,
              g_pre_ffn, g_post_ffn, w_router, b_router, w_mlp1, b_mlp1, w_mlp2, b_mlp2):
    c_act = jax.nn.silu(c)
    for l in range(DEPTH):
        mod = (c_act @ w_mod[l] + b_mod[l])[:, None, :]
        shift1, scale1, gate1, shift2, scale2, gate2 = jnp.split(mod, 6, axis=-1)

        h = rmsnorm(x, g_pre_mix[l]) * (1.0 + scale1) + shift1
        z = h @ w_in[l] + b_in[l]
        q, k, v, u_sg, v_sg, g_att, g_sg = jnp.split(z, SPLIT_POINTS, axis=-1)
        y_att = sliding_window_attention(q, k, v, attn_sinks[l])
        y_sg = chunked_spatial_gating(jax.nn.gelu(u_sg), jax.nn.gelu(v_sg),
                                      sg_ln_g[l], sg_ln_b[l], sg_w[l], sg_b[l])
        merged = (jax.nn.sigmoid(g_att) * (y_att @ w_br_attn[l])
                  + jax.nn.sigmoid(g_sg) * (y_sg @ w_br_sg[l]))
        y = merged @ w_out[l] + b_out[l]
        x = x + gate1 * rmsnorm(y, g_post_mix[l])

        h = rmsnorm(x, g_pre_ffn[l]) * (1.0 + scale2) + shift2
        y = moe_ffn(h, w_router[l], b_router[l], w_mlp1[l], b_mlp1[l], w_mlp2[l], b_mlp2[l])
        x = x + gate2 * rmsnorm(y, g_post_ffn[l])
    return x


_drawn_inputs = setup_inputs


def setup_inputs(seed=0):
    import zlib

    import numpy as np

    out = dict(_drawn_inputs(seed))
    spreads = {}
    factors = {'b_mlp1': 5.979, 'b_mlp2': 8.0}
    for name, (base, spread) in spreads.items():
        noise = np.random.default_rng([zlib.crc32(name.encode()), seed]).standard_normal(out[name].shape)
        drawn = base * np.exp(spread * noise) if base else spread * noise
        out[name] = __import__('jax').numpy.asarray(drawn.astype(out[name].dtype))
    for name, factor in factors.items():
        out[name] = (out[name] * factor).astype(out[name].dtype)
    return out
```

```python
from contextlib import ExitStack

import numpy as np

import concourse.bass as bass
import concourse.mybir as mybir

F32 = mybir.dt.float32
I32 = mybir.dt.int32
ACT = mybir.ActivationFunctionType
ALU = mybir.AluOpType
AX = mybir.AxisListType

P = 128
SEQ, D = 256, 1024
TT = SEQ // P
KT = D // P
HEADS, KV_HEADS, HD = 8, 2, 64
GROUPS, SGW = 8, 512
EXPERTS, TOP_K = 32, 4
BLK = 64
MAX_BLOCKS = SEQ // BLK
ALPHA, LIMIT, EPS = 1.702, 7.0, 1e-6
SLOTS, PIECE = 6, KT * D
FRONT_SLOTS = 3
FAR = 1.0e30
MASKED = -1.0e30
UNROUTED = 10000.0

MOD_EARLY, IN_PIECES, MOD_LATE = [0, 1], [2, 3, 4, 5], [6, 7, 8, 9]
BR_PIECE, OUT_PIECE, FRONT_PIECES = 10, 11, 12

V_BMOD, V_C, V_GPREMIX, V_GPREFFN = 0, 48, 56, 64
V_BQ, V_BK, V_BU, V_BG, V_GPOSTMIX, V_GPOSTFFN, V_ROWS = 72, 76, 77, 81, 97, 105, 113


def layer_program(nc, t, out):
    ctx = ExitStack()
    with ctx:
        def sb(name, shape, dt=F32):
            return ctx.enter_context(nc.sbuf_tensor(name, shape, dt))

        def sem(name):
            return ctx.enter_context(nc.semaphore(name))

        W = sb("weight_slots", [P, SLOTS, KT, D])
        h2 = sb("h2", [P, TT, D])
        ident = sb("ident", [P, P])
        slot_iota = sb("slot_iota", [P, SEQ])
        b1T = sb("b1T", [P, EXPERTS, 16])
        posx = sb("posx", [P, TT, EXPERTS])
        gates = sb("gates", [P, TT, EXPERTS])
        nblk = sb("nblk", [P, EXPERTS], I32)
        sel = sb("sel", [P, TT, BLK])
        gsel = sb("gsel", [P, TT, BLK])
        xg = sb("xg", [P, KT, BLK])
        gbuf = sb("gbuf", [P, KT, BLK])
        sig = sb("sig", [P, KT, BLK])
        lbuf = sb("lbuf", [P, KT, BLK])
        act_sb = sb("act_sb", [P, KT, BLK])
        yT = sb("yT", [P, KT, BLK])
        y_sb = sb("y_sb", [BLK, D])
        gm = sb("gm", [BLK, TT, P])
        small = sb("small", [P, 384])

        U = gbuf[:].rearrange("p k s -> p (k s)")[:, 0:P]
        ones = gbuf[:].rearrange("p k s -> p (k s)")[:, P:2 * P]
        revidx = gbuf[:].rearrange("p k s -> p (k s)")[:, 2 * P:2 * P + EXPERTS]
        wr = lbuf[:].rearrange("p k s -> p (k s)")[:, 0:KT * EXPERTS].rearrange(
            "p (k e) -> p k e", k=KT)
        b2_sb = y_sb[0:EXPERTS, :]
        gT = xg[:].rearrange("p k s -> p (k s)")[0:EXPERTS, 0:SEQ].rearrange(
            "p (t q) -> p t q", t=TT)

        front = W[:, FRONT_SLOTS:SLOTS, :, :].rearrange("p s k n -> p (s k n)")
        place = [0]

        def fb(*dims):
            n = int(np.prod(dims))
            a = front[:, place[0]:place[0] + n]
            place[0] += n
            assert place[0] <= FRONT_SLOTS * PIECE, place[0]
            names = [f"d{i}" for i in range(len(dims))]
            return a if len(dims) == 1 else a.rearrange(
                f"p ({' '.join(names)}) -> p {' '.join(names)}",
                **{n: d for n, d in zip(names, dims)})

        x_sb = fb(TT, D)
        hT = fb(KT, SEQ)
        xn = fb(TT, D)
        at = place[0] - 2 * TT * D
        pT = front[:, at:at + 24 * P].rearrange("p (i q) -> p i q", i=24)
        at = place[0]
        qT = fb(4, SEQ)
        kT, kT_swapped = fb(SEQ), fb(SEQ)
        v_tok = fb(TT, P)
        uT = fb(4, SEQ)
        v_sg = fb(TT, SGW)
        wT = fb(GROUPS, P)
        rows = front[:, at:at + 4 * D].rearrange("p (r n) -> p r n", r=4)
        gate_sig = fb(16, SEQ)
        at = place[0]
        L1 = fb(HEADS, 2 * P)
        L0 = fb(HEADS, P)
        mT = front[:, at:at + KT * SEQ].rearrange("p (k s) -> p k s", k=KT)
        b1_rows = front[:, at:at + 4 * P].rearrange("p (a c) -> p a c", a=4)
        at = place[0]
        yattT = fb(4, SEQ)
        ysgT = fb(4, SEQ)
        sg_rows = front[:, at:at + GROUPS * P].rearrange("p (g s) -> p g s", g=GROUPS)
        dist = fb(2 * P)
        ln_g, ln_b, bias_vsg = fb(SGW), fb(SGW), fb(SGW)
        bias_v = fb(P)
        bias_out = fb(D)
        sg_bias = fb(4, P)
        vec_rows = fb(P)
        vecT = fb(P)
        modT = fb(48)
        branch = fb(SEQ)
        f_small = fb(320)

        fs = [0]

        def fcols(n):
            fs[0] += n
            assert fs[0] <= 320
            return f_small[:, fs[0] - n:fs[0]]

        sumsq, rstd = fcols(TT), fcols(TT)
        sumsq_y, rstd_y = fcols(TT), fcols(TT)
        sumsq_x1, rstd_x1 = fcols(TT), fcols(TT)
        csig, cact = fcols(KT), fcols(KT)
        A1 = fcols(KT)
        row_cols = fcols(4 * KT).rearrange("p (r k) -> p r k", r=4)
        sink8 = fcols(HEADS)
        mx = fcols(2 * HEADS).rearrange("p (b h) -> p b h", b=2)
        negm = fcols(2 * HEADS).rearrange("p (b h) -> p b h", b=2)
        den = fcols(2 * HEADS).rearrange("p (b h) -> p b h", b=2)
        sinkp = fcols(2 * HEADS).rearrange("p (b h) -> p b h", b=2)
        stats = fcols(TT * 6).rearrange("p (t c) -> p t c", t=TT)
        mv = fcols(TT * 2).rearrange("p (t c) -> p t c", t=TT)
        ln_rstd = fcols(TT)

        sm = [0]

        def scols(*dims):
            n = int(np.prod(dims))
            sm[0] += n
            assert sm[0] <= 384
            a = small[:, sm[0] - n:sm[0]]
            return a if len(dims) == 1 else a.rearrange("p (a b) -> p a b", a=dims[0])

        bias_router = scols(EXPERTS)
        lg = scols(TT, EXPERTS)
        picked = scols(TT, EXPERTS)
        chosen = scols(TT, EXPERTS)
        work = scols(TT, EXPERTS)
        top, negtop, rank, gsum = scols(TT), scols(TT), scols(TT), scols(TT)
        blocks_f = scols(EXPERTS)
        sumsq_f, rstd_f = scols(TT), scols(TT)

        banks = ctx.enter_context(nc.psum_tensor("banks", [P, 8, 512], F32))
        big = banks[:, 4:8, :]
        bigf = big.rearrange("p b n -> p (b n)")
        mod_ps = banks[:, 3, 0:48]
        bank_g, bank_l, bank_y, bank_x = (banks[:, b, :] for b in range(4))
        sums = bigf.rearrange("p (t n) -> p t n", t=TT)

        park = nc.dram_tensor("parked", (P, (TT + 1) * D), F32).ap()

        slot_full = [sem(f"slot_full_{s}") for s in range(SLOTS)]
        br_sg_full = sem("br_sg_full")
        x_in, vecs_in, b1_in, sgw_in, cols_in = map(sem, (
            "x_in", "vecs_in", "b1_in", "sgw_in", "cols_in"))
        consts_ready, masked_w = sem("consts_ready"), sem("masked_w")
        dve_step, act_step, pool_step = sem("dve_step"), sem("act_step"), sem("pool_step")
        sq_ready, xn_ready, xnT_full = sem("sq_ready"), sem("xn_ready"), sem("xnT_full")
        cact_ready, csig_ready = sem("cact_ready"), sem("csig_ready")
        k_swapped = sem("k_swapped")
        root_in, root_out = sem("root_in"), sem("root_out")
        mod_full, mod_ready = sem("mod_full"), sem("mod_ready")
        hT_dve, hT_act = sem("hT_dve"), sem("hT_act")
        z_full, z_evac = sem("z_full"), sem("z_evac")
        scores_full, logits_ready, probs_exp, probs_ready = map(sem, (
            "scores_full", "logits_ready", "probs_exp", "probs_ready"))
        negm_ready, sink_exp = sem("negm_ready"), sem("sink_exp")
        pT_full, pT_evac = sem("pT_full"), sem("pT_evac")
        att_full, att_evac = sem("att_full"), sem("att_evac")
        vsg_biased, vsg_gelu, vsg_ready, v_ready = map(sem, (
            "vsg_biased", "vsg_gelu", "vsg_ready", "v_ready"))
        mix_full, ysg_ready = sem("mix_full"), sem("ysg_ready")
        row_cols_ready, rowb_full, rowb_evac = map(sem, (
            "row_cols_ready", "rowb_full", "rowb_evac"))
        br_full, merged_ready = sem("br_full"), sem("merged_ready")
        y_full, y_biased, ysq_ready = sem("y_full"), sem("y_biased"), sem("ysq_ready")
        x1_ready, x1sq_ready, h2_ready = sem("x1_ready"), sem("x1sq_ready"), sem("h2_ready")
        h2T_full, h2T_evac = sem("h2T_full"), sem("h2T_evac")
        logits_full, lg_ready = sem("logits_full"), sem("lg_ready")
        negtop_ready, gexp_ready, chosen_ready = map(sem, (
            "negtop_ready", "gexp_ready", "chosen_ready"))
        pos_full, gates_ready, gT_full, gT_ready = map(sem, (
            "pos_full", "gates_ready", "gT_full", "gT_ready"))
        table_ready, front_done, parked = sem("table_ready"), sem("front_done"), sem("parked")
        sel_ready, gsel_ready, yb_evac, g_evac, g_ready, l_evac, l_ready, gl_ready, act_ready = map(
            sem, ("sel_ready", "gsel_ready", "yb_evac", "g_evac", "g_ready", "l_evac", "l_ready",
                  "gl_ready", "act_ready"))
        xg_ready, ya_evac, sig_ready, gm_ready, yT_ready = map(sem, (
            "xg_ready", "ya_evac", "sig_ready", "gm_ready", "yT_ready"))
        gather_full, ytr_full, g_full, l_full, combined, gm_full, yT_full = map(sem, (
            "gather_full", "ytr_full", "g_full", "l_full", "combined", "gm_full", "yT_full"))
        blocks_over = sem("blocks_over")
        reloaded, fsq_ready, out_ready, out_done = map(sem, (
            "reloaded", "fsq_ready", "out_ready", "out_done"))

        def piece(w):
            return w.rearrange("(k p) n -> p k n", p=P)

        w_mod, w_in = piece(t["w_mod"][0]), piece(t["w_in"][0])
        w_br_attn, w_br_sg = piece(t["w_br_attn"][0]), piece(t["w_br_sg"][0])
        w_out = piece(t["w_out"][0])
        w1 = t["w_mlp1"].rearrange("l e (k p) n -> (l e) p k n", p=P)
        w2 = t["w_mlp2"].rearrange("l e (k p) n -> (l e) p k n", p=P)
        x_dram = t["x"].rearrange("b (t p) n -> p (b t) n", p=P)
        out_dram = out.rearrange("b (t p) n -> p (b t) n", p=P)
        IN_W = t["w_in"].shape[2]

        x1_back = W[:, 0, 0:TT, :]
        row_back = W[:, 0, TT, :]
        y_out = W[:, 1, 0:TT, :]
        fsq_scratch = W[:, 1, TT:2 * TT, :]
        sq_scratch = gate_sig.rearrange("p g s -> p (g s)")[:, 0:TT * D].rearrange(
            "p (t n) -> p t n", t=TT)

        piece_done = [(mod_full, 1), (mod_full, 2), (z_full, 12), (z_full, 18), (z_full, 26),
                      (z_full, 32), (mod_full, 3), (mod_full, 4), (mod_full, 5), (mod_full, 6),
                      (br_full, KT), (y_full, 2 * TT)]

        block = ctx.enter_context(nc.Block())

        @block.sync
        def _(sp):
            for n in range(FRONT_PIECES):
                s = n % FRONT_SLOTS
                if n >= FRONT_SLOTS:
                    sp.wait_ge(*piece_done[n - FRONT_SLOTS])
                if n in MOD_EARLY:
                    sp.dma_start(W[:, s], w_mod[:, :, n * D:(n + 1) * D]).then_inc(slot_full[s], 16)
                elif n in IN_PIECES:
                    a = (n - IN_PIECES[0]) * D
                    b = min(a + D, IN_W)
                    sp.dma_start(W[:, s, :, 0:b - a], w_in[:, :, a:b]).then_inc(slot_full[s], 16)
                elif n in MOD_LATE:
                    a = (n - MOD_LATE[0] + 2) * D
                    sp.dma_start(W[:, s], w_mod[:, :, a:a + D]).then_inc(slot_full[s], 16)
                elif n == BR_PIECE:
                    sp.dma_start(W[:, s, 0:4], w_br_attn).then_inc(slot_full[s], 16)
                    sp.dma_start(W[:, s, 4:8], w_br_sg).then_inc(br_sg_full, 16)
                else:
                    sp.dma_start(W[:, s], w_out).then_inc(slot_full[s], 16)

            def load(e, half, used, value):
                s = 3 * half
                if used is not None:
                    sp.wait_ge(g_full, value)
                sp.dma_start(W[:, s], w1[e, :, :, 0:D]).then_inc(slot_full[s], 16)
                if used is not None:
                    sp.wait_ge(l_full, value)
                sp.dma_start(W[:, s + 1], w1[e, :, :, D:2 * D]).then_inc(slot_full[s + 1], 16)
                if used is not None:
                    sp.wait_ge(yT_full, value)
                sp.dma_start(W[:, s + 2], w2[e]).then_inc(slot_full[s + 2], 16)

            sp.wait_ge(*piece_done[FRONT_PIECES - 3])
            sp.dma_start(W[:, 0], w1[0, :, :, 0:D]).then_inc(slot_full[0], 16)
            sp.wait_ge(*piece_done[FRONT_PIECES - 2])
            sp.dma_start(W[:, 1], w1[0, :, :, D:2 * D]).then_inc(slot_full[1], 16)
            sp.wait_ge(*piece_done[FRONT_PIECES - 1])
            sp.dma_start(W[:, 2], w2[0]).then_inc(slot_full[2], 16)
            sp.wait_ge(x1_ready, TT)
            sp.dma_start(park[:, 0:TT * D], x_sb.rearrange("p t n -> p (t n)")).then_inc(parked, 16)
            sp.wait_ge(rowb_evac, 8)
            sp.dma_start(park[:, TT * D:(TT + 1) * D], rows[:, 3, :]).then_inc(parked, 16)
            sp.wait_ge(parked, 32)
            sp.wait_ge(front_done, 1)
            load(1, 1, None, None)
            sp.wait_ge(table_ready, 1)
            used = sp.alloc_register("blocks_used")
            sp.reg_mov(used, 1)
            with sp.Fori(1, EXPERTS // 2) as i:
                for half in range(2):
                    n = sp.value_load(nblk[0:1, bass.ds(2 * i - 2 + half, 1)],
                                      min_val=1, max_val=MAX_BLOCKS)
                    sp.reg_add(used, used, n)
                    load(2 * i + half, half, used, sp.snap(used))
            n = sp.value_load(nblk[0:1, EXPERTS - 2:EXPERTS - 1], min_val=1, max_val=MAX_BLOCKS)
            sp.reg_add(used, used, n)
            sp.wait_ge(g_full, sp.snap(used))
            sp.dma_start(W[:, 0, 0:TT + 1, :].rearrange("p k n -> p (k n)"),
                         park).then_inc(reloaded, 16)
            for m in range(TT):
                sp.wait_ge(out_ready, m + 1)
                sp.dma_start(out_dram[:, m, :], y_out[:, m, :]).then_inc(out_done, 16)
            sp.wait_ge(out_done, 16 * TT)

        @block.gpsimd
        def _(pool):
            g = nc.gpsimd
            g.memset(ident[:], 0.0).then_inc(pool_step, 1)
            g.memset(ones, 1.0).then_inc(pool_step, 1)
            pool.wait_ge(pool_step, 2)
            g.affine_select(out=ident[:], in_=ident[:], compare_op=ALU.not_equal, fill=1.0, base=0,
                            pattern=[[-1, P]], channel_multiplier=1).then_inc(consts_ready, 1)
            g.iota(dist, [[-1, 2 * P]], base=P, channel_multiplier=1,
                   allow_small_or_imprecise_dtypes=True).then_inc(pool_step, 1)
            pool.wait_ge(pool_step, 3)
            g.affine_select(out=dist, in_=dist, compare_op=ALU.is_ge, fill=FAR, base=P,
                            pattern=[[-1, 2 * P]], channel_multiplier=1).then_inc(pool_step, 1)
            pool.wait_ge(pool_step, 4)
            g.affine_select(out=dist, in_=dist, compare_op=ALU.is_ge, fill=FAR, base=-1,
                            pattern=[[1, 2 * P]], channel_multiplier=-1).then_inc(consts_ready, 1)
            g.affine_select(out=U, in_=ones, compare_op=ALU.is_ge, fill=0.0, base=-1,
                            pattern=[[1, P]], channel_multiplier=-1).then_inc(consts_ready, 1)
            g.iota(slot_iota[:], [[1, SEQ]], base=0, channel_multiplier=0,
                   allow_small_or_imprecise_dtypes=True).then_inc(consts_ready, 1)
            g.iota(revidx, [[-1, EXPERTS]], base=EXPERTS, channel_multiplier=0,
                   allow_small_or_imprecise_dtypes=True).then_inc(consts_ready, 1)
            pool.wait_ge(z_evac, 4)
            g.affine_select(out=wT, in_=wT, compare_op=ALU.is_ge, fill=0.0, base=0,
                            pattern=[[0, GROUPS], [1, P]], channel_multiplier=-1).then_inc(masked_w, 1)

        @block.scalar
        def _(act):
            s = nc.scalar
            for m in range(TT):
                act.dma_start(x_sb[:, m, :], x_dram[:, m, :]).then_inc(x_in, 16)
            b_in = t["b_in"]
            vec_loads = [
                (V_BMOD, 48, t["b_mod"]), (V_C, 8, t["c"]), (V_GPREMIX, 8, t["g_pre_mix"]),
                (V_GPREFFN, 8, t["g_pre_ffn"]), (V_BQ, 4, b_in[:, 0:512]), (V_BK, 1, b_in[:, 512:640]),
                (V_BU, 4, b_in[:, 768:1280]), (V_BG, 16, b_in[:, 1792:3840]),
                (V_GPOSTMIX, 8, t["g_post_mix"]), (V_GPOSTFFN, 8, t["g_post_ffn"])]
            for r, n, v in vec_loads:
                act.dma_start(vec_rows[r:r + n, :], v.rearrange("a (r c) -> (a r) c", c=P)
                              ).then_inc(vecs_in, 16)
            act.dma_start(b1_rows, t["b_mlp1"].rearrange("l e (m c) -> (l e m) c", c=P).rearrange(
                "(a r) c -> r a c", r=P)).then_inc(b1_in, 16)
            act.dma_start(sg_rows, t["sg_w"].rearrange("l g t s -> t (l g) s")).then_inc(sgw_in, 16)
            for dst, src in ((bias_v, b_in[:, 640:768]), (bias_vsg, b_in[:, 1280:1792]),
                             (ln_g, t["sg_ln_g"]), (ln_b, t["sg_ln_b"]), (bias_out, t["b_out"]),
                             (bias_router, t["b_router"]), (sink8, t["attn_sinks"])):
                act.dma_start(dst, src.to_broadcast([P, src.shape[1]])).then_inc(cols_in, 16)
            for half in range(2):
                act.dma_start(sg_bias[half * HD:(half + 1) * HD],
                              t["sg_b"].rearrange("l (j h) t -> (l h) j t", h=2)[half:half + 1]
                              .to_broadcast([HD, 4, P])).then_inc(cols_in, 16)
            act.dma_start(wr, t["w_router"][0].rearrange("(k p) e -> p k e", p=P)).then_inc(cols_in, 16)
            act.dma_start(b2_sb, t["b_mlp2"][0]).then_inc(cols_in, 16)

            for m in range(TT):
                act.wait_ge(x_in, 16 * TT)
                s.activation(xn[:, m, :], x_sb[:, m, :], ACT.Square,
                             accum_out=sumsq[:, m:m + 1]).then_inc(sq_ready, 1)

            def root(n, dst):
                act.wait_ge(root_in, n + 1)
                s.activation(dst, dst, ACT.Sqrt).then_inc(root_out, 1)

            root(0, rstd)

            act.wait_ge(z_full, 1)
            s.copy(vecT[:, 0:V_ROWS], banks[:, 0, 0:V_ROWS]).then_inc(z_evac, 1)
            act.wait_ge(z_evac, 1)
            s.activation(csig, vecT[:, V_C:V_C + KT], ACT.Sigmoid).then_inc(csig_ready, 1)
            act.wait_ge(z_full, 2)
            s.copy(b1T[:].rearrange("p e m -> p (e m)"), banks[:, 1, :]).then_inc(z_evac, 1)
            for half in range(2):
                act.wait_ge(z_full, 3 + half)
                s.copy(wT[:, 4 * half:4 * half + 4, :],
                       banks[:, (2 + half) % 3, :].rearrange("p (g t) -> p g t", g=4)
                       ).then_inc(z_evac, 1)

            act.wait_ge(xnT_full, 1)
            act.wait_ge(mod_ready, 2)
            for k in range(KT // 2, KT):
                last = s.activation(hT[:, k, :], bigf[:, k * SEQ:(k + 1) * SEQ], ACT.Identity,
                                    bias=modT[:, k:k + 1], scale=A1[:, k:k + 1])
            last.then_inc(hT_act, 1)

            def z_tile(r, dst, width, func, bias):
                act.wait_ge(z_full, r + 1)
                src = banks[:, r % 3, 0:width]
                if bias is None:
                    s.copy(dst, src).then_inc(z_evac, 1)
                else:
                    s.activation(dst, src, func, bias=bias).then_inc(z_evac, 1)

            def gate_tile(j):
                z_tile(16 + j, gate_sig[:, j, :], SEQ, ACT.Sigmoid, vecT[:, V_BG + j:V_BG + j + 1])

            def exps(b, L):
                act.wait_ge(negm_ready, 2 * b + 1)
                for h in range(HEADS):
                    last = s.activation(L[:, h, :], L[:, h, :], ACT.Exp, scale=0.125,
                                        bias=negm[:, b, h:h + 1], accum_out=den[:, b, h:h + 1])
                last.then_inc(probs_exp, 1)
                act.wait_ge(negm_ready, 2 * b + 2)
                s.activation(sinkp[:, b, :], sinkp[:, b, :], ACT.Exp).then_inc(sink_exp, 1)

            for j in range(4):
                z_tile(4 + j, qT[:, j, :], SEQ, ACT.Identity, vecT[:, V_BQ + j:V_BQ + j + 1])
            z_tile(8, kT, SEQ, ACT.Identity, vecT[:, V_BK:V_BK + 1])
            act.wait_ge(z_evac, 9)
            s.copy(kT_swapped[0:HD, :], kT[HD:P, :])
            s.copy(kT_swapped[HD:P, :], kT[0:HD, :]).then_inc(k_swapped, 1)
            z_tile(9, v_tok.rearrange("p t c -> p (t c)"), SEQ, None, None)
            for j in range(4):
                z_tile(10 + j, uT[:, j, :], SEQ, ACT.Gelu_apprx_tanh, vecT[:, V_BU + j:V_BU + j + 1])
            for m in range(TT):
                z_tile(14 + m, v_sg[:, m, :], SGW, None, None)
            act.wait_ge(vsg_biased, TT)
            for m in range(TT):
                s.activation(v_sg[:, m, :], v_sg[:, m, :], ACT.Gelu_apprx_tanh).then_inc(vsg_gelu, 1)
            for j in range(2):
                gate_tile(j)
            exps(0, L1)
            exps(1, L0)
            root(1, ln_rstd)
            for j in range(2, 16):
                gate_tile(j)

            for r in range(3):
                act.wait_ge(pT_full, r + 1)
                b = 2 * (r % 2)
                s.copy(pT[:, 8 * r:8 * r + 8, :].rearrange("p i q -> p (i q)"),
                       bigf[:, b * 512:(b + 2) * 512]).then_inc(pT_evac, 1)
            act.wait_ge(att_full, 1)
            s.copy(yattT.rearrange("p j s -> p (j s)"), bigf[:, 1024:2048]).then_inc(att_evac, 1)

            for i in range(8):
                act.wait_ge(rowb_full, i + 1)
                if i == 0:
                    act.wait_ge(ysg_ready, 1)
                s.copy(rows[:, i // 2, (i % 2) * 512:(i % 2 + 1) * 512],
                       banks[:, i % 3, :]).then_inc(rowb_evac, 1)

            for m in range(TT):
                act.wait_ge(y_biased, 2 * m + 2)
                s.activation(sq_scratch[:, m, :], xn[:, m, :], ACT.Square,
                             accum_out=sumsq_y[:, m:m + 1]).then_inc(ysq_ready, 1)
            root(2, rstd_y)
            for m in range(TT):
                act.wait_ge(x1_ready, m + 1)
                s.activation(sq_scratch[:, m, :], x_sb[:, m, :], ACT.Square,
                             accum_out=sumsq_x1[:, m:m + 1]).then_inc(x1sq_ready, 1)
            root(3, rstd_x1)
            act.wait_ge(h2T_full, 1)
            s.copy(hT.rearrange("p k s -> p (k s)"), bigf).then_inc(h2T_evac, 1)
            act.wait_ge(negtop_ready, 1)
            for m in range(TT):
                last = s.activation(gates[:, m, :], lg[:, m, :], ACT.Exp, bias=negtop[:, m:m + 1])
            last.then_inc(gexp_ready, 1)
            act.wait_ge(gT_full, 1)
            s.copy(gT.rearrange("p t q -> p (t q)"),
                   banks[0:EXPERTS, 2, 0:SEQ]).then_inc(gT_ready, 1)

            for done in (xg_ready, ya_evac, sig_ready):
                act.sem_inc(done, 1)
            act.wait_ge(table_ready, 1)
            blk = act.alloc_register("act_block")
            act.reg_mov(blk, 1)
            with act.Fori(0, EXPERTS) as e:
                n = act.value_load(nblk[0:1, bass.ds(e, 1)], min_val=1, max_val=MAX_BLOCKS)
                with act.Fori(0, n) as _c:
                    prev = act.snap(blk)
                    this = act.snap(prev + 1)
                    act.wait_ge(gather_full, this)
                    act.wait_ge(l_full, prev)
                    s.copy(xg[:].rearrange("p k s -> p (k s)"), bank_x).then_inc(xg_ready, 1)
                    act.wait_ge(ytr_full, this)
                    act.wait_ge(combined, prev)
                    s.copy(y_sb[:, 0:512], bank_y[0:BLK, :]).then_inc(ya_evac, 1)
                    act.wait_ge(g_ready, this)
                    s.activation(sig[:].rearrange("p k s -> p (k s)"),
                                 gbuf[:].rearrange("p k s -> p (k s)"),
                                 ACT.Sigmoid, scale=ALPHA).then_inc(sig_ready, 1)
                    act.wait_ge(gm_full, this)
                    act.wait_ge(combined, this)
                    s.copy(gm[:].rearrange("p t q -> p (t q)"),
                           bank_x[0:BLK, 0:SEQ]).then_inc(gm_ready, 1)
                    act.wait_ge(yT_full, this)
                    act.wait_ge(ytr_full, this)
                    s.copy(yT[:].rearrange("p k s -> p (k s)"), bank_y).then_inc(yT_ready, 1)
                    act.reg_add(blk, blk, 1)
            total = act.snap(blk)
            act.wait_ge(ytr_full, total + 1)
            act.wait_ge(combined, total)
            s.copy(y_sb[:, 0:512], bank_y[0:BLK, :]).then_inc(ya_evac, 1)
            act.wait_ge(combined, total + 1)
            act.wait_ge(reloaded, 16)
            for m in range(TT):
                s.activation(fsq_scratch[:, m, :], sums[:, m, :], ACT.Square,
                             accum_out=sumsq_f[:, m:m + 1]).then_inc(fsq_ready, 1)
            root(4, rstd_f)

        @block.vector
        def _(dve):
            v = nc.vector
            steps = [0]

            def link(ins):
                steps[0] += 1
                ins.then_inc(dve_step, 1)
                dve.wait_ge(dve_step, steps[0])

            roots = [0]

            def rstd_of(dst, sq, n):
                link(v.tensor_scalar(dst, sq, 1.0 / n, EPS, ALU.mult, ALU.add))
                v.reciprocal(dst, dst).then_inc(root_in, 1)
                roots[0] += 1
                dve.wait_ge(root_out, roots[0])

            v.memset(yT[:], 0.0).then_inc(yT_ready, 1)
            v.memset(gm[:], 0.0).then_inc(gm_ready, 1)

            dve.wait_ge(sq_ready, TT)
            rstd_of(rstd, sumsq, D)
            for m in range(TT):
                v.tensor_scalar(xn[:, m, :], x_sb[:, m, :], rstd[:, m:m + 1], None,
                                ALU.mult).then_inc(xn_ready, 1)
            dve.wait_ge(csig_ready, 1)
            v.tensor_tensor(cact, vecT[:, V_C:V_C + KT], csig, ALU.mult).then_inc(cact_ready, 1)
            dve.wait_ge(mod_full, 2)
            v.tensor_tensor(modT[:, 0:16], mod_ps[:, 0:16], vecT[:, 0:16],
                            ALU.add).then_inc(mod_ready, 1)
            dve.wait_ge(mod_ready, 1)
            v.scalar_tensor_tensor(out=A1, in0=modT[:, 8:16], scalar=1.0,
                                   in1=vecT[:, V_GPREMIX:V_GPREMIX + KT],
                                   op0=ALU.add, op1=ALU.mult).then_inc(mod_ready, 1)
            dve.wait_ge(mod_ready, 2)
            dve.wait_ge(xnT_full, 1)
            for k in range(KT // 2):
                last = v.tensor_scalar(hT[:, k, :], bigf[:, k * SEQ:(k + 1) * SEQ], A1[:, k:k + 1],
                                       modT[:, k:k + 1], ALU.mult, ALU.add)
            last.then_inc(hT_dve, 1)
            dve.wait_ge(cols_in, 16 * 11)
            link(v.tensor_scalar(sink8, sink8, 8.0, None, ALU.mult))
            dve.wait_ge(z_evac, 10)
            v.tensor_tensor(v_tok, v_tok, bias_v.unsqueeze(1).to_broadcast([P, TT, P]),
                            ALU.add).then_inc(v_ready, 1)

            def logits(b, L, src, dist_b):
                dve.wait_ge(scores_full, b + 1)
                for h in range(HEADS):
                    slope = 2.0 ** (-8.0 * (h + 1) / HEADS)
                    last = v.scalar_tensor_tensor(out=L[:, h, :], in0=dist_b, scalar=-8.0 * slope,
                                                  in1=src[:, (h % 2) * 4 + h // 2, :], op0=ALU.mult, op1=ALU.add)
                last.then_inc(logits_ready, 1)
                dve.wait_ge(logits_ready, b + 1)
                link(v.tensor_reduce(mx[:, b, :], L, AX.X, ALU.max))
                link(v.tensor_tensor(mx[:, b, :], mx[:, b, :], sink8, ALU.max))
                v.tensor_scalar(negm[:, b, :], mx[:, b, :], -0.125, None,
                                ALU.mult).then_inc(negm_ready, 1)
                dve.wait_ge(negm_ready, 2 * b + 1)
                v.scalar_tensor_tensor(out=sinkp[:, b, :], in0=sink8, scalar=0.125,
                                       in1=negm[:, b, :], op0=ALU.mult,
                                       op1=ALU.add).then_inc(negm_ready, 1)

            def probs(b, L, width):
                dve.wait_ge(probs_exp, b + 1)
                dve.wait_ge(sink_exp, b + 1)
                link(v.tensor_tensor(den[:, b, :], den[:, b, :], sinkp[:, b, :], ALU.add))
                link(v.reciprocal(den[:, b, :], den[:, b, :]))
                v.tensor_tensor(L, L, den[:, b, :].unsqueeze(2).to_broadcast([P, HEADS, width]),
                                ALU.mult).then_inc(probs_ready, 1)

            dve.wait_ge(consts_ready, 2)
            logits(0, L1, bigf.rearrange("p (h k) -> p h k", h=HEADS), dist)
            dve.wait_ge(z_evac, 16)
            for m in range(TT):
                v.tensor_tensor(v_sg[:, m, :], v_sg[:, m, :], bias_vsg,
                                ALU.add).then_inc(vsg_biased, 1)
            logits(1, L0, bigf[:, 0:1024].rearrange("p (h k) -> p h k", h=HEADS), dist[:, P:2 * P])
            for m in range(TT):
                dve.wait_ge(vsg_gelu, m + 1)
                link(v.bn_stats(stats[:, m, :], v_sg[:, m, :]))
                link(v.bn_aggr(mv[:, m, :], stats[:, m, :]))
            rstd_of(ln_rstd, mv[:, :, 1], 1)
            for m in range(TT):
                link(v.tensor_scalar(v_sg[:, m, :], v_sg[:, m, :], mv[:, m, 0:1],
                                     ln_rstd[:, m:m + 1], ALU.subtract, ALU.mult))
                link(v.tensor_tensor(v_sg[:, m, :], v_sg[:, m, :], ln_g, ALU.mult))
                v.tensor_tensor(v_sg[:, m, :], v_sg[:, m, :], ln_b, ALU.add).then_inc(vsg_ready, 1)
            probs(0, L1, 2 * P)
            probs(1, L0, P)

            dve.wait_ge(mix_full, 1)
            link(v.tensor_tensor(
                ysgT.rearrange("p j (b q) -> p j b q", b=2),
                bigf[:, 0:1024].rearrange("p (j b q) -> p j b q", j=4, b=2),
                sg_bias.unsqueeze(2).to_broadcast([P, 4, 2, P]), ALU.add))
            v.tensor_tensor(ysgT, ysgT, uT, ALU.mult).then_inc(ysg_ready, 1)

            dve.wait_ge(mod_full, 6)
            link(v.tensor_tensor(modT[:, 16:48], mod_ps[:, 16:48], vecT[:, 16:48], ALU.add))
            v.tensor_tensor(row_cols[:, 0, :], modT[:, 16:24], vecT[:, V_GPOSTMIX:V_GPOSTMIX + KT],
                            ALU.mult)
            v.scalar_tensor_tensor(out=row_cols[:, 1, :], in0=modT[:, 32:40], scalar=1.0,
                                   in1=vecT[:, V_GPREFFN:V_GPREFFN + KT], op0=ALU.add, op1=ALU.mult)
            v.tensor_copy(row_cols[:, 2, :], modT[:, 24:32])
            v.tensor_tensor(row_cols[:, 3, :], modT[:, 40:48],
                            vecT[:, V_GPOSTFFN:V_GPOSTFFN + KT], ALU.mult).then_inc(row_cols_ready, 1)

            for n in range(KT):
                dve.wait_ge(br_full, n + 1)
                if n:
                    dve.wait_ge(merged_ready, n)
                src = banks[:, n % 3, :]
                v.tensor_tensor(mT[:, n, :], src[:, 0:SEQ], gate_sig[:, n, :],
                                ALU.mult).then_inc(dve_step, 1)
                v.tensor_tensor(branch, src[:, SEQ:2 * SEQ], gate_sig[:, 8 + n, :],
                                ALU.mult).then_inc(dve_step, 1)
                steps[0] += 2
                dve.wait_ge(dve_step, steps[0])
                v.tensor_tensor(mT[:, n, :], mT[:, n, :], branch, ALU.add).then_inc(merged_ready, 1)

            for m in range(TT):
                for h in range(2):
                    dve.wait_ge(y_full, 2 * m + h + 1)
                    c = slice(h * 512, (h + 1) * 512)
                    v.tensor_tensor(xn[:, m, c], sums[:, m, c], bias_out[:, c],
                                    ALU.add).then_inc(y_biased, 1)
            dve.wait_ge(ysq_ready, TT)
            rstd_of(rstd_y, sumsq_y, D)
            dve.wait_ge(rowb_evac, 8)
            for m in range(TT):
                link(v.scalar_tensor_tensor(out=xn[:, m, :], in0=xn[:, m, :],
                                            scalar=rstd_y[:, m:m + 1], in1=rows[:, 0, :],
                                            op0=ALU.mult, op1=ALU.mult))
                v.tensor_tensor(x_sb[:, m, :], x_sb[:, m, :], xn[:, m, :],
                                ALU.add).then_inc(x1_ready, 1)
            dve.wait_ge(x1sq_ready, TT)
            rstd_of(rstd_x1, sumsq_x1, D)
            for m in range(TT):
                link(v.scalar_tensor_tensor(out=h2[:, m, :], in0=x_sb[:, m, :],
                                            scalar=rstd_x1[:, m:m + 1], in1=rows[:, 1, :],
                                            op0=ALU.mult, op1=ALU.mult))
                v.tensor_tensor(h2[:, m, :], h2[:, m, :], rows[:, 2, :],
                                ALU.add).then_inc(h2_ready, 1)

            dve.wait_ge(logits_full, 1)
            v.tensor_tensor(lg, banks[:, 0, 0:TT * EXPERTS].rearrange("p (t e) -> p t e", t=TT),
                            bias_router.unsqueeze(1).to_broadcast([P, TT, EXPERTS]),
                            ALU.add).then_inc(lg_ready, 1)
            dve.wait_ge(lg_ready, 1)
            dve.sem_inc(front_done, 1)
            link(v.tensor_copy(work, lg))
            wide = [P, TT, EXPERTS]
            for r in range(TOP_K):
                link(v.tensor_reduce(top, work, AX.X, ALU.max))
                if r == 0:
                    v.tensor_scalar(negtop, top, -1.0, None, ALU.mult).then_inc(negtop_ready, 1)
                link(v.tensor_tensor(picked, work, top.unsqueeze(2).to_broadcast(wide),
                                     ALU.is_equal))
                link(v.tensor_tensor(picked, picked, revidx.unsqueeze(1).to_broadcast(wide),
                                     ALU.mult))
                link(v.tensor_reduce(rank, picked, AX.X, ALU.max))
                link(v.tensor_tensor(picked, revidx.unsqueeze(1).to_broadcast(wide),
                                     rank.unsqueeze(2).to_broadcast(wide), ALU.is_equal))
                if r == 0:
                    link(v.tensor_copy(chosen, picked))
                else:
                    link(v.tensor_tensor(chosen, chosen, picked, ALU.add))
                if r < TOP_K - 1:
                    link(v.scalar_tensor_tensor(out=work, in0=picked, scalar=MASKED, in1=work,
                                                op0=ALU.mult, op1=ALU.add))
            dve.sem_inc(chosen_ready, 1)
            dve.wait_ge(gexp_ready, 1)
            link(v.tensor_tensor(gates[:], gates[:], chosen, ALU.mult))
            link(v.tensor_reduce(gsum, gates[:], AX.X, ALU.add))
            link(v.reciprocal(gsum, gsum))
            v.tensor_tensor(gates[:], gates[:], gsum.unsqueeze(2).to_broadcast(wide),
                            ALU.mult).then_inc(gates_ready, 1)
            dve.wait_ge(pos_full, 1)
            pos_ps = banks[:, 1, 0:3 * EXPERTS].rearrange("p (t e) -> p t e", t=3)
            link(v.tensor_scalar(posx[:], pos_ps[:, 0:TT, :], UNROUTED, None, ALU.add))
            link(v.scalar_tensor_tensor(out=posx[:], in0=chosen, scalar=-UNROUTED, in1=posx[:],
                                        op0=ALU.mult, op1=ALU.add))
            link(v.tensor_scalar(blocks_f, pos_ps[:, 2, :], BLK + 0.5, 1.0, ALU.is_gt, ALU.add))
            for j in range(2, MAX_BLOCKS):
                link(v.scalar_tensor_tensor(out=blocks_f, in0=pos_ps[:, 2, :],
                                            scalar=BLK * j + 0.5, in1=blocks_f,
                                            op0=ALU.is_gt, op1=ALU.add))
            v.tensor_copy(nblk[:], blocks_f).then_inc(table_ready, 1)

            for done in (yb_evac, g_evac, l_evac):
                dve.sem_inc(done, 1)
            for done in (sel_ready, gsel_ready, g_ready, l_ready, gl_ready, act_ready):
                dve.sem_inc(done, 1)
            dve.wait_ge(table_ready, 1)
            dve.wait_ge(gates_ready, 1)
            blk = dve.alloc_register("dve_block")
            dve.reg_mov(blk, 1)
            wide_e = [P, KT, BLK]
            flat = "p k s -> p (k s)"
            with dve.Fori(0, EXPERTS) as e:
                n = dve.value_load(nblk[0:1, bass.ds(e, 1)], min_val=1, max_val=MAX_BLOCKS)
                with dve.Fori(0, n) as c:
                    prev = dve.snap(blk)
                    this = dve.snap(prev + 1)
                    dve.wait_ge(gm_full, prev)
                    dve.wait_ge(gather_full, prev)
                    for m in range(TT):
                        last = v.tensor_scalar(sel[:, m, :], slot_iota[:, bass.ds(c * BLK, BLK)],
                                               posx[:, m, bass.ds(e, 1)], None, ALU.is_equal)
                    last.then_inc(sel_ready, 1)
                    dve.wait_ge(sel_ready, this)
                    for m in range(TT):
                        last = v.tensor_scalar(gsel[:, m, :], sel[:, m, :],
                                               gates[:, m, bass.ds(e, 1)], None, ALU.mult)
                    last.then_inc(gsel_ready, 1)
                    dve.wait_ge(ytr_full, this)
                    dve.wait_ge(combined, prev)
                    v.tensor_copy(y_sb[:, 512:1024], bank_l[0:BLK, :]).then_inc(yb_evac, 1)
                    dve.wait_ge(g_full, this)
                    v.tensor_tensor(gbuf[:], bank_g.rearrange("p (k s) -> p k s", k=KT),
                                    b1T[:, bass.ds(e, 1), 0:KT].rearrange("p a m -> p (a m)")
                                    .unsqueeze(2).to_broadcast(wide_e),
                                    ALU.add).then_inc(g_evac, 1)
                    dve.wait_ge(g_evac, this)
                    v.tensor_scalar(gbuf[:].rearrange(flat), gbuf[:].rearrange(flat), LIMIT, None,
                                    ALU.min).then_inc(g_ready, 1)
                    dve.wait_ge(l_full, this)
                    v.tensor_tensor(lbuf[:], bank_l.rearrange("p (k s) -> p k s", k=KT),
                                    b1T[:, bass.ds(e, 1), KT:2 * KT].rearrange("p a m -> p (a m)")
                                    .unsqueeze(2).to_broadcast(wide_e),
                                    ALU.add).then_inc(l_evac, 1)
                    dve.wait_ge(l_evac, this)
                    v.tensor_scalar(lbuf[:].rearrange(flat), lbuf[:].rearrange(flat), LIMIT, -LIMIT,
                                    ALU.min, ALU.max).then_inc(l_ready, 1)
                    dve.wait_ge(l_ready, this)
                    v.scalar_tensor_tensor(out=lbuf[:].rearrange(flat), in0=lbuf[:].rearrange(flat),
                                           scalar=1.0, in1=gbuf[:].rearrange(flat), op0=ALU.add,
                                           op1=ALU.mult).then_inc(gl_ready, 1)
                    dve.wait_ge(gl_ready, this)
                    dve.wait_ge(sig_ready, this)
                    dve.wait_ge(yT_full, prev)
                    v.tensor_tensor(act_sb[:].rearrange(flat), lbuf[:].rearrange(flat),
                                    sig[:].rearrange(flat), ALU.mult).then_inc(act_ready, 1)
                    dve.reg_add(blk, blk, 1)
            total = dve.snap(blk)
            dve.wait_ge(ytr_full, total + 1)
            dve.wait_ge(combined, total)
            v.tensor_copy(y_sb[:, 512:1024], bank_l[0:BLK, :]).then_inc(yb_evac, 1)
            dve.wait_ge(fsq_ready, TT)
            rstd_of(rstd_f, sumsq_f, D)
            dve.wait_ge(reloaded, 16)
            for m in range(TT):
                link(v.scalar_tensor_tensor(out=y_out[:, m, :], in0=sums[:, m, :],
                                            scalar=rstd_f[:, m:m + 1], in1=row_back,
                                            op0=ALU.mult, op1=ALU.mult))
                v.tensor_tensor(y_out[:, m, :], y_out[:, m, :], x1_back[:, m, :],
                                ALU.add).then_inc(out_ready, 1)

        @block.tensor
        def _(pe):
            mm, tr = nc.tensor.matmul, nc.tensor.transpose

            def piece_in(n):
                pe.wait_ge(slot_full[n % FRONT_SLOTS], 16 * (n // FRONT_SLOTS + 1))
                return W[:, n % FRONT_SLOTS]

            pe.wait_ge(consts_ready, 1)
            pe.wait_ge(vecs_in, 16 * 10)
            tr(banks[:, 0, 0:V_ROWS], vec_rows[0:V_ROWS, :],
               ident[0:V_ROWS, 0:V_ROWS]).then_inc(z_full, 1)
            pe.wait_ge(b1_in, 16)
            for a in range(4):
                last = tr(banks[:, 1, a * P:(a + 1) * P], b1_rows[:, a, :], ident[:])
            last.then_inc(z_full, 1)
            pe.wait_ge(sgw_in, 16)
            for half in range(2):
                if half:
                    pe.wait_ge(z_evac, 1)
                for g in range(4):
                    last = tr(banks[:, (2 + half) % 3, g * P:(g + 1) * P],
                              sg_rows[:, 4 * half + g, :], ident[:])
                last.then_inc(z_full, 1)
            pe.wait_ge(xn_ready, TT)
            for k in range(KT):
                for m in range(TT):
                    last = tr(bigf[:, k * SEQ + m * P:k * SEQ + (m + 1) * P],
                              xn[:, m, k * P:(k + 1) * P], ident[:])
            last.then_inc(xnT_full, 1)

            def modulation(i, n):
                w = piece_in(n)
                for m in range(KT):
                    for k in range(KT):
                        last = mm(mod_ps[:, 8 * i + m:8 * i + m + 1], w[:, k, m * P:(m + 1) * P],
                                  cact[:, k:k + 1], start=(k == 0), stop=(k == KT - 1))
                last.then_inc(mod_full, 1)

            pe.wait_ge(cact_ready, 1)
            for n in MOD_EARLY:
                modulation(n, n)
            pe.wait_ge(hT_dve, 1)
            pe.wait_ge(hT_act, 1)

            def z_bank(r):
                pe.wait_ge(z_evac, r - 2)
                return banks[:, r % 3, :]

            def z_transposed(r, w, cols):
                b = z_bank(r)
                for k in range(KT):
                    last = mm(b[:, 0:SEQ], w[:, k, cols], hT[:, k, :], start=(k == 0),
                              stop=(k == KT - 1))
                last.then_inc(z_full, 1)

            w = piece_in(IN_PIECES[0])
            for j in range(4):
                z_transposed(4 + j, w, slice(j * P, (j + 1) * P))
            z_transposed(8, w, slice(512, 640))
            b = z_bank(9)
            for m in range(TT):
                for k in range(KT):
                    last = mm(b[:, m * P:(m + 1) * P], hT[:, k, m * P:(m + 1) * P],
                              w[:, k, 640:768], start=(k == 0), stop=(k == KT - 1))
            last.then_inc(z_full, 1)
            for j in range(2):
                z_transposed(10 + j, w, slice(768 + j * P, 768 + (j + 1) * P))

            def scores(b, width):
                pe.wait_ge(z_evac, 9)
                pe.wait_ge(k_swapped, 1)
                q = slice(P, 2 * P) if b == 0 else slice(0, P)
                for h in range(HEADS):
                    part = slice((h % 2) * HD, (h % 2 + 1) * HD)
                    keys = kT if h % 2 == h // 4 else kT_swapped
                    at = ((h % 2) * 4 + h // 2) * width
                    last = mm(bigf[:, at:at + width], qT[part, h // 2, q],
                              keys[part, 0:width], start=True, stop=True)
                last.then_inc(scores_full, 1)

            scores(0, 2 * P)
            w = piece_in(IN_PIECES[1])
            for j in range(2):
                z_transposed(12 + j, w, slice(j * P, (j + 1) * P))
            for m in range(TT):
                b = z_bank(14 + m)
                for k in range(KT):
                    last = mm(b, hT[:, k, m * P:(m + 1) * P], w[:, k, 256:768], start=(k == 0),
                              stop=(k == KT - 1))
                last.then_inc(z_full, 1)
            for j in range(2):
                z_transposed(16 + j, w, slice(768 + j * P, 768 + (j + 1) * P))
            pe.wait_ge(logits_ready, 1)
            scores(1, P)
            w = piece_in(IN_PIECES[2])
            for j in range(8):
                z_transposed(18 + j, w, slice(j * P, (j + 1) * P))
            w = piece_in(IN_PIECES[3])
            for j in range(6):
                z_transposed(26 + j, w, slice(j * P, (j + 1) * P))

            pe.wait_ge(probs_ready, 2)
            tiles = [L0[:, h, :] for h in range(HEADS)] + [
                L1[:, h, kb * P:(kb + 1) * P] for h in range(HEADS) for kb in range(2)]
            for r in range(3):
                if r == 0:
                    pe.wait_ge(logits_ready, 2)
                if r == 2:
                    pe.wait_ge(pT_evac, 1)
                b = 1024 * (r % 2)
                for i in range(8):
                    last = tr(bigf[:, b + i * P:b + (i + 1) * P], tiles[8 * r + i], ident[:])
                last.then_inc(pT_full, 1)
                if r == 1:
                    modulation(2, MOD_LATE[0])
            modulation(3, MOD_LATE[1])
            pe.wait_ge(v_ready, 1)
            pe.wait_ge(pT_evac, 3)
            for h in range(HEADS):
                vh = slice((h // 4) * HD, (h // 4 + 1) * HD)
                rows_h = slice((h % 2) * HD, (h % 2 + 1) * HD)
                at = 1024 + (h // 2) * SEQ
                mm(bigf[rows_h, at:at + P], v_tok[:, 0, vh], pT[:, h, :], start=True, stop=True)
                for kb in range(2):
                    last = mm(bigf[rows_h, at + P:at + 2 * P], v_tok[:, kb, vh],
                              pT[:, 8 + 2 * h + kb, :], start=(kb == 0), stop=(kb == 1))
            last.then_inc(att_full, 1)
            pe.wait_ge(vsg_ready, TT)
            pe.wait_ge(masked_w, 1)
            for g in range(GROUPS):
                rows_g = slice((g % 2) * HD, (g % 2 + 1) * HD)
                for m in range(TT):
                    at = (g // 2) * SEQ + m * P
                    last = mm(bigf[rows_g, at:at + P], v_sg[:, m, g * HD:(g + 1) * HD], wT[:, g, :],
                              start=True, stop=True)
            last.then_inc(mix_full, 1)
            modulation(4, MOD_LATE[2])
            modulation(5, MOD_LATE[3])

            pe.wait_ge(row_cols_ready, 1)
            pe.wait_ge(z_evac, 32)
            for i in range(8):
                if i >= 3:
                    pe.wait_ge(rowb_evac, i - 2)
                for q in range(4):
                    k = (i % 2) * 4 + q
                    last = mm(banks[:, i % 3, q * P:(q + 1) * P],
                              row_cols[:, i // 2, k:k + 1].to_broadcast([P, P]), ident[:],
                              start=True, stop=True)
                last.then_inc(rowb_full, 1)

            w = piece_in(BR_PIECE)
            pe.wait_ge(br_sg_full, 16)
            pe.wait_ge(att_evac, 1)
            pe.wait_ge(ysg_ready, 1)
            pe.wait_ge(rowb_evac, 8)
            for n in range(KT):
                if n >= 3:
                    pe.wait_ge(merged_ready, n - 2)
                for side, src in ((0, yattT), (1, ysgT)):
                    for k in range(4):
                        last = mm(banks[:, n % 3, side * SEQ:(side + 1) * SEQ],
                                  w[:, 4 * side + k, n * P:(n + 1) * P], src[:, k, :],
                                  start=(k == 0), stop=(k == 3))
                last.then_inc(br_full, 1)
            w = piece_in(OUT_PIECE)
            pe.wait_ge(merged_ready, KT)
            for m in range(TT):
                for h in range(2):
                    c = slice(h * 512, (h + 1) * 512)
                    for k in range(KT):
                        last = mm(sums[:, m, c], mT[:, k, m * P:(m + 1) * P], w[:, k, c],
                                  start=(k == 0), stop=(k == KT - 1))
                    last.then_inc(y_full, 1)

            pe.wait_ge(y_biased, 4)
            pe.wait_ge(h2_ready, TT)
            for k in range(KT):
                for m in range(TT):
                    last = tr(bigf[:, k * SEQ + m * P:k * SEQ + (m + 1) * P],
                              h2[:, m, k * P:(k + 1) * P], ident[:])
            last.then_inc(h2T_full, 1)
            pe.wait_ge(h2T_evac, 1)
            for m in range(TT):
                for k in range(KT):
                    last = mm(banks[:, 0, m * EXPERTS:(m + 1) * EXPERTS],
                              hT[:, k, m * P:(m + 1) * P], wr[:, k, :], start=(k == 0),
                              stop=(k == KT - 1))
            last.then_inc(logits_full, 1)
            pe.wait_ge(chosen_ready, 1)
            pe.wait_ge(consts_ready, 5)
            E = EXPERTS
            mm(banks[:, 1, 0:E], U, chosen[:, 0, :], start=True, stop=True)
            mm(banks[:, 1, E:2 * E], ones, chosen[:, 0, :], start=True, stop=False)
            mm(banks[:, 1, E:2 * E], U, chosen[:, 1, :], start=False, stop=True)
            mm(banks[:, 1, 2 * E:3 * E], ones, chosen[:, 0, :], start=True, stop=False)
            mm(banks[:, 1, 2 * E:3 * E], ones, chosen[:, 1, :], start=False,
               stop=True).then_inc(pos_full, 1)
            pe.wait_ge(gates_ready, 1)
            for m in range(TT):
                last = tr(banks[0:E, 2, m * P:(m + 1) * P], gates[:, m, :], ident[:])
            last.then_inc(gT_full, 1)
            pe.wait_ge(gT_ready, 1)
            for m in range(TT):
                for h in range(2):
                    c = slice(h * 512, (h + 1) * 512)
                    mm(sums[:, m, c], gT[:, m, :], b2_sb[:, c], start=True, stop=False,
                       skip_group_check=True)

            for done in (gather_full, g_full, l_full, combined, gm_full, yT_full, ytr_full):
                pe.sem_inc(done, 1)
            pe.wait_ge(table_ready, 1)
            blk = pe.alloc_register("pe_block")
            pe.reg_mov(blk, 1)

            def turn_result():
                for k in range(KT):
                    b = bank_y if k < 4 else bank_l
                    last = tr(b[0:BLK, (k % 4) * P:(k % 4 + 1) * P], yT[:, k, :], ident[:])
                last.then_inc(ytr_full, 1)

            def combine(stop):
                for m in range(TT):
                    for h in range(2):
                        c = slice(h * 512, (h + 1) * 512)
                        last = mm(sums[:, m, c], gm[:, m, :], y_sb[:, c], start=False, stop=stop,
                                  skip_group_check=True)
                last.then_inc(combined, 1)

            def layer(bank, w, rhs, full):
                for m in range(KT):
                    for k in range(KT):
                        last = mm(bank[:, m * BLK:(m + 1) * BLK], w[:, k, m * P:(m + 1) * P],
                                  rhs[:, k, :], start=(k == 0), stop=(k == KT - 1))
                last.then_inc(full, 1)

            def expert_block(base, full):
                prev = pe.snap(blk)
                this = pe.snap(prev + 1)
                pe.wait_ge(sel_ready, this)
                pe.wait_ge(gm_ready, prev)
                for k in range(KT):
                    if k == KT // 2:
                        pe.wait_ge(l_evac, prev)
                        pe.wait_ge(yT_ready, prev)
                    for m in range(TT):
                        last = mm(bank_x[:, k * BLK:(k + 1) * BLK], h2[:, m, k * P:(k + 1) * P],
                                  sel[:, m, :], start=(m == 0), stop=(m == TT - 1))
                last.then_inc(gather_full, 1)
                turn_result()
                pe.wait_ge(xg_ready, this)
                pe.wait_ge(g_evac, prev)
                pe.wait_ge(slot_full[base], full)
                layer(bank_g, W[:, base], xg, g_full)
                pe.wait_ge(yb_evac, this)
                pe.wait_ge(slot_full[base + 1], full)
                layer(bank_l, W[:, base + 1], xg, l_full)
                pe.wait_ge(gsel_ready, this)
                pe.wait_ge(ya_evac, this)
                combine(False)
                for m in range(TT):
                    last = tr(bank_x[0:BLK, m * P:(m + 1) * P], gsel[:, m, :], ident[:])
                last.then_inc(gm_full, 1)
                pe.wait_ge(act_ready, this)
                pe.wait_ge(slot_full[base + 2], full)
                layer(bank_y, W[:, base + 2], act_sb, yT_full)
                pe.reg_add(blk, blk, 1)

            with pe.Fori(0, EXPERTS // 2) as i:
                for half in range(2):
                    n = pe.value_load(nblk[0:1, bass.ds(2 * i + half, 1)], min_val=1,
                                      max_val=MAX_BLOCKS)
                    first = FRONT_PIECES // FRONT_SLOTS + 1 if half == 0 else 1
                    full = pe.snap(16 * i + 16 * first)
                    with pe.Fori(0, n) as _c:
                        expert_block(3 * half, full)
            total = pe.snap(blk)
            pe.wait_ge(yT_ready, total)
            pe.wait_ge(gm_ready, total)
            pe.wait_ge(l_evac, total)
            pe.sem_inc(blocks_over, 1)
            turn_result()
            pe.wait_ge(ya_evac, total + 1)
            pe.wait_ge(yb_evac, total + 1)
            combine(True)


_INS = ["x", "c", "w_mod", "b_mod", "g_pre_mix", "g_post_mix", "w_in", "b_in", "attn_sinks",
        "sg_ln_g", "sg_ln_b", "sg_w", "sg_b", "w_br_attn", "w_br_sg", "w_out", "b_out",
        "g_pre_ffn", "g_post_ffn", "w_router", "b_router", "w_mlp1", "b_mlp1", "w_mlp2", "b_mlp2"]


def kernel(**inputs):
    import concourse.bacc as bacc
    from concourse.bass_utils import run_bass_kernel_spmd

    nc = bacc.Bacc("TRN2", target_bir_lowering=False, num_devices=1, dynamic_dma_scratch_size=64)
    arrays, t = {}, {}
    for name in _INS:
        a = np.ascontiguousarray(inputs[name])
        arrays[name] = a
        t[name] = nc.dram_tensor(name, a.shape, F32, kind="ExternalInput").ap()
    out = nc.dram_tensor("out", (1, SEQ, D), F32, kind="ExternalOutput").ap()
    layer_program(nc, t, out)
    r = run_bass_kernel_spmd(nc, [arrays], core_ids=[0])
    return r.results[0]["out"]
```

```python
from contextlib import ExitStack

import numpy as np

import concourse.bass as bass
import concourse.mybir as mybir

F32 = mybir.dt.float32
I32 = mybir.dt.int32
ACT = mybir.ActivationFunctionType
ALU = mybir.AluOpType
AX = mybir.AxisListType

P = 128
SEQ, D = 256, 1024
TT = SEQ // P
KT = D // P
HEADS, KV_HEADS, HD = 8, 2, 64
GROUPS, SGW = 8, 512
EXPERTS, TOP_K = 32, 4
BLK = 32
MAX_BLOCKS = SEQ // BLK
HALF = 512
NQ, QW = 4, D // 4
QUARTER = 32
ALPHA, LIMIT, EPS = 1.702, 7.0, 1e-6
SLOTS, PIECE = 6, KT * D
FRONT_SLOTS = 3
FAR = 1.0e30
MASKED = -1.0e30
UNROUTED = 10000.0

MOD_EARLY, IN_PIECES, MOD_LATE = [0, 1], [2, 3, 4, 5], [6, 7, 8, 9]
BR_PIECE, OUT_PIECE, FRONT_PIECES = 10, 11, 12

V_C, V_GPREMIX, V_BQ, V_BK, V_BU, V_BG, V_ROWS = 0, 8, 16, 20, 21, 25, 41


def layer_program(nc, t, out):
    ctx = ExitStack()
    with ctx:
        def sb(name, shape, dt=F32):
            return ctx.enter_context(nc.sbuf_tensor(name, shape, dt))

        def sem(name):
            return ctx.enter_context(nc.semaphore(name))

        W = sb("weight_slots", [P, SLOTS, KT, D])
        h2 = sb("h2", [P, TT, D])
        ident = sb("ident", [P, P])
        slot_iota = sb("slot_iota", [P, SEQ])
        b1q = sb("b1q", [P, HALF])
        posx = sb("posx", [P, TT, EXPERTS])
        gates = sb("gates", [P, TT, EXPERTS])
        nblk = sb("nblk", [P, EXPERTS], I32)
        sel = sb("sel", [P, TT, BLK])
        gsel = sb("gsel", [P, TT, NQ, BLK])
        bsel = sb("bsel", [P, 4, BLK])
        work_sb = sb("work_sb", [P, 7, QW])
        xg_rows, xgT, gbuf, sig, lbuf, actT, y_sb = (work_sb[:, i, :] for i in range(7))
        gm = sb("gm", [P, TT, P])
        mod_late = sb("mod_late", [P, 2, HALF])
        post_rows = sb("post_rows", [P, 2, HALF])
        small = sb("small", [P, 384])

        work_flat = work_sb[:].rearrange("p a b -> p (a b)")
        U, ones = work_flat[:, 0:P], work_flat[:, P:2 * P]
        gT = work_flat[0:EXPERTS, 256:512].rearrange("p (t q) -> p t q", t=TT)
        lgT = work_flat[0:EXPERTS, 256:512]
        wr = work_flat[:, 512:768].rearrange("p (k e) -> p k e", k=KT)
        b2_sb = work_flat[0:EXPERTS, 768:1792]

        front = W[:, FRONT_SLOTS:SLOTS, :, :].rearrange("p s k n -> p (s k n)")
        place = [0]

        def fb(*dims):
            n = int(np.prod(dims))
            a = front[:, place[0]:place[0] + n]
            place[0] += n
            assert place[0] <= FRONT_SLOTS * PIECE, place[0]
            names = [f"d{i}" for i in range(len(dims))]
            return a if len(dims) == 1 else a.rearrange(
                f"p ({' '.join(names)}) -> p {' '.join(names)}",
                **{n: d for n, d in zip(names, dims)})

        x_sb = fb(TT, D)
        hT = fb(KT, SEQ)
        xn = fb(TT, D)
        at = place[0] - 2 * TT * D
        pT = front[:, at:at + 24 * P].rearrange("p (i q) -> p i q", i=24)
        at = place[0]
        qT = fb(4, SEQ)
        kT, kT_swapped = fb(SEQ), fb(SEQ)
        v_tok = fb(TT, P)
        uT = fb(4, SEQ)
        v_sg = fb(TT, SGW)
        wT = fb(GROUPS, P)
        rows = front[:, at:at + 4 * D].rearrange("p (r n) -> p r n", r=4)
        gate_sig = fb(16, SEQ)
        at = place[0]
        L1 = fb(HEADS, 2 * P)
        L0 = fb(HEADS, P)
        mT = front[:, at:at + KT * SEQ].rearrange("p (k s) -> p k s", k=KT)
        mod_early = front[:, at:at + HALF]
        at = place[0]
        yattT = fb(4, SEQ)
        ysgT = fb(4, SEQ)
        sg_rows = front[:, at:at + GROUPS * P].rearrange("p (g s) -> p g s", g=GROUPS)
        dist = fb(2 * P)
        ln_g, ln_b, bias_vsg = fb(SGW), fb(SGW), fb(SGW)
        bias_v = fb(P)
        bias_out = fb(D)
        sg_bias = fb(4, P)
        vec_rows = fb(P)
        vecT = fb(P)
        modT = fb(16)
        branch = fb(SEQ)
        f_small = fb(320)

        fs = [0]

        def fcols(n):
            fs[0] += n
            assert fs[0] <= 320
            return f_small[:, fs[0] - n:fs[0]]

        sumsq, rstd = fcols(TT), fcols(TT)
        sumsq_y, rstd_y = fcols(TT), fcols(TT)
        sumsq_x1, rstd_x1 = fcols(TT), fcols(TT)
        csig, cact = fcols(KT), fcols(KT)
        A1 = fcols(KT)
        sink8 = fcols(HEADS)
        mx = fcols(2 * HEADS).rearrange("p (b h) -> p b h", b=2)
        negm = fcols(2 * HEADS).rearrange("p (b h) -> p b h", b=2)
        den = fcols(2 * HEADS).rearrange("p (b h) -> p b h", b=2)
        sinkp = fcols(2 * HEADS).rearrange("p (b h) -> p b h", b=2)
        stats = fcols(TT * 6).rearrange("p (t c) -> p t c", t=TT)
        mv = fcols(TT * 2).rearrange("p (t c) -> p t c", t=TT)
        ln_rstd = fcols(TT)

        sm = [0]

        def scols(*dims):
            n = int(np.prod(dims))
            sm[0] += n
            assert sm[0] <= 384
            a = small[:, sm[0] - n:sm[0]]
            return a if len(dims) == 1 else a.rearrange("p (a b) -> p a b", a=dims[0])

        bias_router = scols(EXPERTS)
        revidx = scols(EXPERTS)
        lg = scols(TT, EXPERTS)
        picked = scols(TT, EXPERTS)
        chosen = scols(TT, EXPERTS)
        work = scols(TT, EXPERTS)
        top, negtop, rank, gsum = scols(TT), scols(TT), scols(TT), scols(TT)
        blocks_f = scols(EXPERTS)
        sumsq_f, rstd_f = scols(TT), scols(TT)

        banks = ctx.enter_context(nc.psum_tensor("banks", [P, 8, 512], F32))
        big = banks[:, 4:8, :]
        bigf = big.rearrange("p b n -> p (b n)")
        mod_ps = banks[:, 3, :]
        bank_g, bank_l, bank_y, bank_x = (banks[:, b, 0:QW] for b in range(4))
        turned_g = bank_g
        y_ps = bigf.rearrange("p (t n) -> p t n", t=TT)
        sums = big.rearrange("p q (t n) -> p q t n", t=TT)

        park = nc.dram_tensor("parked", (P, (TT + 1) * D), F32).ap()

        slot_full = [sem(f"slot_full_{s}") for s in range(SLOTS)]
        br_sg_full = sem("br_sg_full")
        distance_ready = sem("distance_ready")
        early_issued, rest_issued = sem("early_issued"), sem("rest_issued")
        x_in, vecs_in, bmod_in, sgw_in, cols_in = map(sem, (
            "x_in", "vecs_in", "bmod_in", "sgw_in", "cols_in"))
        consts_ready, masked_w = sem("consts_ready"), sem("masked_w")
        dve_step, act_step, pool_step = sem("dve_step"), sem("act_step"), sem("pool_step")
        sq_ready, xn_ready, xnT_full = sem("sq_ready"), sem("xn_ready"), sem("xnT_full")
        cact_ready, csig_ready = sem("cact_ready"), sem("csig_ready")
        k_swapped = sem("k_swapped")
        root_in, root_out = sem("root_in"), sem("root_out")
        mod_full, mod_ready = sem("mod_full"), sem("mod_ready")
        mod_evac, modT_full, late_in, lgT_full, lgT_ready = map(sem, (
            "mod_evac", "modT_full", "late_in", "lgT_full", "lgT_ready"))
        hT_dve, hT_act = sem("hT_dve"), sem("hT_act")
        z_full, z_evac = sem("z_full"), sem("z_evac")
        scores_full, logits_ready, probs_exp, probs_ready = map(sem, (
            "scores_full", "logits_ready", "probs_exp", "probs_ready"))
        negm_ready, sink_exp = sem("negm_ready"), sem("sink_exp")
        pT_full, pT_evac = sem("pT_full"), sem("pT_evac")
        att_full, att_evac = sem("att_full"), sem("att_evac")
        vsg_biased, vsg_gelu, vsg_ready, v_ready = map(sem, (
            "vsg_biased", "vsg_gelu", "vsg_ready", "v_ready"))
        mix_full, ysg_ready = sem("mix_full"), sem("ysg_ready")
        mod_rows_ready, rowb_full, rowb_evac = map(sem, (
            "mod_rows_ready", "rowb_full", "rowb_evac"))
        br_full, merged_ready = sem("br_full"), sem("merged_ready")
        y_full, y_biased, ysq_ready = sem("y_full"), sem("y_biased"), sem("ysq_ready")
        x1_ready, x1sq_ready, h2_ready = sem("x1_ready"), sem("x1sq_ready"), sem("h2_ready")
        h2T_full, h2T_evac = sem("h2T_full"), sem("h2T_evac")
        logits_full, lg_ready = sem("logits_full"), sem("lg_ready")
        negtop_ready, gexp_ready, chosen_ready = map(sem, (
            "negtop_ready", "gexp_ready", "chosen_ready"))
        pos_full, gates_ready, gT_full, gT_ready = map(sem, (
            "pos_full", "gates_ready", "gT_full", "gT_ready"))
        b2_used = sem("b2_used")
        table_ready, front_done, parked = sem("table_ready"), sem("front_done"), sem("parked")
        sel_ready, gsel_ready, bsel_ready, pool_waits, g_ready, l_ready, gl_ready, act_ready = map(
            sem, ("sel_ready", "gsel_ready", "bsel_ready", "pool_waits", "g_ready", "l_ready",
                  "gl_ready", "act_ready"))
        xg_evac, xgT_ready, gm_ready, sig_ready, actT_ready, res_ready = map(sem, (
            "xg_evac", "xgT_ready", "gm_ready", "sig_ready", "actT_ready", "res_ready"))
        gather_full, xturn_full, gm_full, g_full, l_full, aturn_full, res_full, combined = map(
            sem, ("gather_full", "xturn_full", "gm_full", "g_full", "l_full", "aturn_full",
                  "res_full", "combined"))
        reloaded, fsq_ready, out_ready, out_done = map(sem, (
            "reloaded", "fsq_ready", "out_ready", "out_done"))

        def piece(w):
            return w.rearrange("(k p) n -> p k n", p=P)

        w_mod, w_in = piece(t["w_mod"][0]), piece(t["w_in"][0])
        w_br_attn, w_br_sg = piece(t["w_br_attn"][0]), piece(t["w_br_sg"][0])
        w_out = piece(t["w_out"][0])
        w1 = t["w_mlp1"].rearrange("l e (k p) n -> (l e) p k n", p=P)
        w2 = t["w_mlp2"].rearrange("l e (k p) n -> (l e) p k n", p=P)
        x_dram = t["x"].rearrange("b (t p) n -> p (b t) n", p=P)
        out_dram = out.rearrange("b (t p) n -> p (b t) n", p=P)
        IN_W = t["w_in"].shape[2]

        x1_back = W[:, 0, 0:TT, :]
        row_back = W[:, 0, TT, :]
        y_out = W[:, 1, 0:TT, :]
        fsq_scratch = W[:, 1, TT:2 * TT, :]
        sq_scratch = gate_sig.rearrange("p g s -> p (g s)")[:, 0:TT * D].rearrange(
            "p (t n) -> p t n", t=TT)

        piece_done = [(mod_full, 1), (mod_full, 2), (z_full, 11), (z_full, 17), (z_full, 25),
                      (z_full, 31), (mod_full, 3), (mod_full, 4), (mod_full, 5), (mod_full, 6),
                      (br_full, KT), (y_full, 2 * TT)]

        block = ctx.enter_context(nc.Block())

        @block.sync
        def _(sp):
            for n in range(FRONT_PIECES):
                s = n % FRONT_SLOTS
                if n >= FRONT_SLOTS:
                    sp.wait_ge(*piece_done[n - FRONT_SLOTS])
                if n == 1:
                    sp.wait_ge(early_issued, 1)
                if n == 2:
                    sp.wait_ge(rest_issued, 1)
                if n in MOD_EARLY:
                    sp.dma_start(W[:, s], w_mod[:, :, n * D:(n + 1) * D]).then_inc(slot_full[s], 16)
                elif n in IN_PIECES:
                    a = (n - IN_PIECES[0]) * D
                    b = min(a + D, IN_W)
                    sp.dma_start(W[:, s, :, 0:b - a], w_in[:, :, a:b]).then_inc(slot_full[s], 16)
                elif n in MOD_LATE:
                    a = (n - MOD_LATE[0] + 2) * D
                    sp.dma_start(W[:, s], w_mod[:, :, a:a + D]).then_inc(slot_full[s], 16)
                elif n == BR_PIECE:
                    sp.dma_start(W[:, s, 0:4], w_br_attn).then_inc(slot_full[s], 16)
                    sp.dma_start(W[:, s, 4:8], w_br_sg).then_inc(br_sg_full, 16)
                else:
                    sp.dma_start(W[:, s], w_out).then_inc(slot_full[s], 16)

            def load(e, half, used, value):
                s = 3 * half
                if used is not None:
                    sp.wait_ge(g_full, value)
                sp.dma_start(W[:, s], w1[e, :, :, 0:D]).then_inc(slot_full[s], 16)
                if used is not None:
                    sp.wait_ge(l_full, value)
                sp.dma_start(W[:, s + 1], w1[e, :, :, D:2 * D]).then_inc(slot_full[s + 1], 16)
                if used is not None:
                    sp.wait_ge(res_full, value)
                sp.dma_start(W[:, s + 2], w2[e]).then_inc(slot_full[s + 2], 16)

            sp.wait_ge(*piece_done[FRONT_PIECES - 3])
            sp.dma_start(W[:, 0], w1[0, :, :, 0:D]).then_inc(slot_full[0], 16)
            sp.wait_ge(*piece_done[FRONT_PIECES - 2])
            sp.dma_start(W[:, 1], w1[0, :, :, D:2 * D]).then_inc(slot_full[1], 16)
            sp.wait_ge(*piece_done[FRONT_PIECES - 1])
            sp.dma_start(W[:, 2], w2[0]).then_inc(slot_full[2], 16)
            sp.wait_ge(x1_ready, TT)
            sp.dma_start(park[:, 0:TT * D], x_sb.rearrange("p t n -> p (t n)")).then_inc(parked, 16)
            sp.wait_ge(rowb_evac, 4)
            sp.dma_start(park[:, TT * D:(TT + 1) * D], rows[:, 3, :]).then_inc(parked, 16)
            sp.wait_ge(parked, 32)
            sp.wait_ge(front_done, 1)
            load(1, 1, None, None)
            sp.wait_ge(table_ready, 1)
            used = sp.alloc_register("blocks_used")
            sp.reg_mov(used, 1)
            with sp.Fori(1, EXPERTS // 2) as i:
                for half in range(2):
                    n = sp.value_load(nblk[0:1, bass.ds(2 * i - 2 + half, 1)],
                                      min_val=1, max_val=MAX_BLOCKS)
                    sp.reg_add(used, used, n)
                    load(2 * i + half, half, used, sp.snap(used))
            n = sp.value_load(nblk[0:1, EXPERTS - 2:EXPERTS - 1], min_val=1, max_val=MAX_BLOCKS)
            sp.reg_add(used, used, n)
            sp.wait_ge(g_full, sp.snap(used))
            sp.dma_start(W[:, 0, 0:TT + 1, :].rearrange("p k n -> p (k n)"),
                         park).then_inc(reloaded, 16)
            for m in range(TT):
                sp.wait_ge(out_ready, m + 1)
                sp.dma_start(out_dram[:, m, :], y_out[:, m, :]).then_inc(out_done, 16)
            sp.wait_ge(out_done, 16 * TT)

        @block.gpsimd
        def _(pool):
            g = nc.gpsimd
            g.memset(ident[:], 0.0).then_inc(pool_step, 1)
            g.memset(ones, 1.0).then_inc(pool_step, 1)
            pool.wait_ge(pool_step, 2)
            g.affine_select(out=ident[:], in_=ident[:], compare_op=ALU.not_equal, fill=1.0, base=0,
                            pattern=[[-1, P]], channel_multiplier=1).then_inc(consts_ready, 1)
            g.iota(dist, [[-1, 2 * P]], base=P, channel_multiplier=1,
                   allow_small_or_imprecise_dtypes=True).then_inc(pool_step, 1)
            pool.wait_ge(pool_step, 3)
            g.affine_select(out=dist, in_=dist, compare_op=ALU.is_ge, fill=FAR, base=P,
                            pattern=[[-1, 2 * P]], channel_multiplier=1).then_inc(pool_step, 1)
            pool.wait_ge(pool_step, 4)
            g.affine_select(out=dist, in_=dist, compare_op=ALU.is_ge, fill=FAR, base=-1,
                            pattern=[[1, 2 * P]], channel_multiplier=-1).then_inc(consts_ready, 1)
            g.affine_select(out=U, in_=ones, compare_op=ALU.is_ge, fill=0.0, base=-1,
                            pattern=[[1, P]], channel_multiplier=-1).then_inc(consts_ready, 1)
            g.iota(slot_iota[:], [[1, SEQ]], base=0, channel_multiplier=0,
                   allow_small_or_imprecise_dtypes=True).then_inc(consts_ready, 1)
            g.iota(revidx, [[-1, EXPERTS]], base=EXPERTS, channel_multiplier=0,
                   allow_small_or_imprecise_dtypes=True).then_inc(consts_ready, 1)
            pool.wait_ge(z_evac, 3)
            g.affine_select(out=wT, in_=wT, compare_op=ALU.is_ge, fill=0.0, base=0,
                            pattern=[[0, GROUPS], [1, P]], channel_multiplier=-1).then_inc(masked_w, 1)

            for done in (sel_ready, gsel_ready, bsel_ready):
                pool.sem_inc(done, 1)
            pool.wait_ge(table_ready, 1)
            pool.wait_ge(gates_ready, 1)
            blk = pool.alloc_register("pool_block")
            pool.reg_mov(blk, 1)
            with pool.Fori(0, EXPERTS) as e:
                n = pool.value_load(nblk[0:1, bass.ds(e, 1)], min_val=1, max_val=MAX_BLOCKS)
                with pool.Fori(0, n) as c:
                    prev = pool.snap(blk)
                    this = pool.snap(prev + 1)
                    pool.wait_ge(gather_full, prev)
                    pool.wait_ge(gsel_ready, prev)
                    pool.sem_inc(pool_waits, 1)
                    for m in range(TT):
                        last = g.tensor_tensor(
                            sel[:, m, :], slot_iota[:, bass.ds(c * BLK, BLK)],
                            posx[:, m, bass.ds(e, 1)].to_broadcast([P, BLK]), ALU.subtract)
                    last.then_inc(distance_ready, 1)
                    pool.wait_ge(distance_ready, prev)
                    pool.sem_inc(pool_waits, 1)
                    g.tensor_scalar(sel[:], sel[:], 0.0, None, ALU.is_equal).then_inc(sel_ready, 1)
                    pool.wait_ge(gm_full, prev)
                    pool.wait_ge(sel_ready, this)
                    pool.sem_inc(pool_waits, 1)
                    for m in range(TT):
                        last = g.tensor_tensor(
                            gsel[:, m], sel[:, m:m + 1, :].to_broadcast([P, NQ, BLK]),
                            gates[:, m, bass.ds(e, 1)].unsqueeze(2).to_broadcast([P, NQ, BLK]),
                            ALU.mult)
                    last.then_inc(gsel_ready, 1)
                    pool.wait_ge(l_full, prev)
                    pool.sem_inc(pool_waits, 1)
                    g.tensor_copy(bsel[:], ident[:, bass.ds(4 * e, 4)].unsqueeze(2)
                                  .to_broadcast([P, 4, BLK])).then_inc(bsel_ready, 1)
                    pool.reg_add(blk, blk, 1)
            total = pool.snap(blk)
            pool.wait_ge(gather_full, total)
            pool.wait_ge(gsel_ready, total)
            pool.sem_inc(pool_waits, 1)
            g.memset(sel[:], 0.0).then_inc(sel_ready, 1)

        @block.scalar
        def _(act):
            s = nc.scalar

            def spread_rows(dst, src, done):
                for r in range(src.shape[0] // HALF):
                    act.dma_start(dst[r * QUARTER:(r + 1) * QUARTER, :],
                                  src[r * HALF:(r + 1) * HALF].unsqueeze(0).to_broadcast(
                                      [QUARTER, HALF])).then_inc(done, 16)

            for m in range(TT):
                act.dma_start(x_sb[:, m, :], x_dram[:, m, :]).then_inc(x_in, 16)
            b_in = t["b_in"]
            vec_loads = [
                (V_C, 8, t["c"]), (V_GPREMIX, 8, t["g_pre_mix"]),
                (V_BQ, 4, b_in[:, 0:512]), (V_BK, 1, b_in[:, 512:640]),
                (V_BU, 4, b_in[:, 768:1280]), (V_BG, 16, b_in[:, 1792:3840])]
            for r, n, v in vec_loads:
                act.dma_start(vec_rows[r:r + n, :], v.rearrange("a (r c) -> (a r) c", c=P)
                              ).then_inc(vecs_in, 16)
            b_mod, row4 = t["b_mod"][0], 4 * HALF
            spread_rows(mod_early, b_mod[0:row4], bmod_in)
            act.sem_inc(early_issued, 1)
            act.dma_start(sg_rows, t["sg_w"].rearrange("l g t s -> t (l g) s")).then_inc(sgw_in, 16)
            for dst, src in ((bias_v, b_in[:, 640:768]), (bias_vsg, b_in[:, 1280:1792]),
                             (ln_g, t["sg_ln_g"]), (ln_b, t["sg_ln_b"]), (bias_out, t["b_out"]),
                             (bias_router, t["b_router"]), (sink8, t["attn_sinks"])):
                act.dma_start(dst, src.to_broadcast([P, src.shape[1]])).then_inc(cols_in, 16)
            for half in range(2):
                act.dma_start(sg_bias[half * HD:(half + 1) * HD],
                              t["sg_b"].rearrange("l (j h) t -> (l h) j t", h=2)[half:half + 1]
                              .to_broadcast([HD, 4, P])).then_inc(cols_in, 16)
            act.dma_start(wr, t["w_router"][0].rearrange("(k p) e -> p k e", p=P)).then_inc(cols_in, 16)
            act.dma_start(b2_sb, t["b_mlp2"][0]).then_inc(cols_in, 16)
            act.dma_start(b1q[:], t["b_mlp1"].rearrange("l e (n c) -> (l e n) c", c=HALF)
                          ).then_inc(cols_in, 16)
            spread_rows(mod_late[:, 0, :], b_mod[row4:2 * row4], late_in)
            spread_rows(mod_late[:, 1, :], b_mod[2 * row4:3 * row4], late_in)
            spread_rows(post_rows[:, 0, :], t["g_post_mix"][0], late_in)
            spread_rows(post_rows[0:2 * QUARTER, 1, :], t["g_pre_ffn"][0], late_in)
            spread_rows(post_rows[2 * QUARTER:P, 1, :], t["g_post_ffn"][0], late_in)
            act.sem_inc(rest_issued, 1)

            for m in range(TT):
                act.wait_ge(x_in, 16 * TT)
                s.activation(xn[:, m, :], x_sb[:, m, :], ACT.Square,
                             accum_out=sumsq[:, m:m + 1]).then_inc(sq_ready, 1)

            def root(n, dst):
                act.wait_ge(root_in, n + 1)
                s.activation(dst, dst, ACT.Sqrt).then_inc(root_out, 1)

            root(0, rstd)

            act.wait_ge(z_full, 1)
            s.copy(vecT[:, 0:V_ROWS], banks[:, 0, 0:V_ROWS]).then_inc(z_evac, 1)
            act.wait_ge(z_evac, 1)
            s.activation(csig, vecT[:, V_C:V_C + KT], ACT.Sigmoid).then_inc(csig_ready, 1)
            for half in range(2):
                act.wait_ge(z_full, 2 + half)
                s.copy(wT[:, 4 * half:4 * half + 4, :],
                       banks[:, 1 + half, :].rearrange("p (g t) -> p g t", g=4)
                       ).then_inc(z_evac, 1)
            act.wait_ge(modT_full, 1)
            s.copy(modT.rearrange("p (r j) -> p r j", r=4),
                   mod_ps.rearrange("p (j r q) -> p r j q", j=4, r=4)[:, :, :, 0]
                   ).then_inc(mod_ready, 1)

            act.wait_ge(xnT_full, 1)
            act.wait_ge(mod_ready, 2)
            for k in range(KT // 2, KT):
                last = s.activation(hT[:, k, :], bigf[:, k * SEQ:(k + 1) * SEQ], ACT.Identity,
                                    bias=modT[:, k:k + 1], scale=A1[:, k:k + 1])
            last.then_inc(hT_act, 1)

            def z_tile(r, dst, width, func, bias):
                act.wait_ge(z_full, r + 1)
                src = banks[:, r % 3, 0:width]
                if bias is None:
                    s.copy(dst, src).then_inc(z_evac, 1)
                else:
                    s.activation(dst, src, func, bias=bias).then_inc(z_evac, 1)

            def gate_tile(j):
                z_tile(15 + j, gate_sig[:, j, :], SEQ, ACT.Sigmoid, vecT[:, V_BG + j:V_BG + j + 1])

            def exps(b, L):
                act.wait_ge(negm_ready, 2 * b + 1)
                for h in range(HEADS):
                    last = s.activation(L[:, h, :], L[:, h, :], ACT.Exp, scale=0.125,
                                        bias=negm[:, b, h:h + 1], accum_out=den[:, b, h:h + 1])
                last.then_inc(probs_exp, 1)
                act.wait_ge(negm_ready, 2 * b + 2)
                s.activation(sinkp[:, b, :], sinkp[:, b, :], ACT.Exp).then_inc(sink_exp, 1)

            for j in range(4):
                z_tile(3 + j, qT[:, j, :], SEQ, ACT.Identity, vecT[:, V_BQ + j:V_BQ + j + 1])
            z_tile(7, kT, SEQ, ACT.Identity, vecT[:, V_BK:V_BK + 1])
            act.wait_ge(z_evac, 8)
            s.copy(kT_swapped[0:HD, :], kT[HD:P, :])
            s.copy(kT_swapped[HD:P, :], kT[0:HD, :]).then_inc(k_swapped, 1)
            z_tile(8, v_tok.rearrange("p t c -> p (t c)"), SEQ, None, None)
            for j in range(4):
                z_tile(9 + j, uT[:, j, :], SEQ, ACT.Gelu_apprx_tanh, vecT[:, V_BU + j:V_BU + j + 1])
            for m in range(TT):
                z_tile(13 + m, v_sg[:, m, :], SGW, None, None)
            act.wait_ge(vsg_biased, TT)
            for m in range(TT):
                s.activation(v_sg[:, m, :], v_sg[:, m, :], ACT.Gelu_apprx_tanh).then_inc(vsg_gelu, 1)
            for j in range(2):
                gate_tile(j)
            exps(0, L1)
            exps(1, L0)
            root(1, ln_rstd)
            for j in range(2, 16):
                gate_tile(j)

            for r in range(3):
                act.wait_ge(pT_full, r + 1)
                b = 2 * (r % 2)
                s.copy(pT[:, 8 * r:8 * r + 8, :].rearrange("p i q -> p (i q)"),
                       bigf[:, b * 512:(b + 2) * 512]).then_inc(pT_evac, 1)
            act.wait_ge(att_full, 1)
            s.copy(yattT.rearrange("p j s -> p (j s)"), bigf[:, 1024:2048]).then_inc(att_evac, 1)

            for i in range(2):
                act.wait_ge(rowb_full, i + 1)
                act.wait_ge(ysg_ready, 1)
                for j, r in enumerate(((0, 2), (1, 3))[i]):
                    s.copy(rows[:, r, :], bigf[:, j * D:(j + 1) * D]).then_inc(rowb_evac, 1)

            for m in range(TT):
                act.wait_ge(y_biased, 2 * m + 2)
                s.activation(sq_scratch[:, m, :], xn[:, m, :], ACT.Square,
                             accum_out=sumsq_y[:, m:m + 1]).then_inc(ysq_ready, 1)
                root(2 + 2 * m, rstd_y[:, m:m + 1])
                act.wait_ge(x1_ready, m + 1)
                s.activation(sq_scratch[:, m, :], x_sb[:, m, :], ACT.Square,
                             accum_out=sumsq_x1[:, m:m + 1]).then_inc(x1sq_ready, 1)
                root(3 + 2 * m, rstd_x1[:, m:m + 1])
            act.wait_ge(h2T_full, 1)
            s.copy(hT.rearrange("p k s -> p (k s)"), bigf).then_inc(h2T_evac, 1)
            act.wait_ge(lgT_full, 1)
            s.copy(lgT, banks[0:EXPERTS, 0, 0:SEQ]).then_inc(lgT_ready, 1)
            act.wait_ge(negtop_ready, 1)
            for m in range(TT):
                last = s.activation(gates[:, m, :], lg[:, m, :], ACT.Exp, bias=negtop[:, m:m + 1])
            last.then_inc(gexp_ready, 1)
            act.wait_ge(gT_full, 1)
            s.copy(gT.rearrange("p t q -> p (t q)"),
                   banks[0:EXPERTS, 3, 0:SEQ]).then_inc(gT_ready, 1)

            for done in (xg_evac, xgT_ready, sig_ready, actT_ready):
                act.sem_inc(done, 1)
            act.wait_ge(table_ready, 1)
            blk = act.alloc_register("act_block")
            act.reg_mov(blk, 1)

            def gathered(count, read):
                act.wait_ge(gather_full, count)
                act.wait_ge(xturn_full, read)
                s.copy(xg_rows, bank_x).then_inc(xg_evac, 1)
                act.wait_ge(xturn_full, count)
                act.wait_ge(l_full, read)
                s.copy(xgT, bank_y).then_inc(xgT_ready, 1)

            gathered(2, 1)
            with act.Fori(0, EXPERTS) as e:
                n = act.value_load(nblk[0:1, bass.ds(e, 1)], min_val=1, max_val=MAX_BLOCKS)
                with act.Fori(0, n) as _c:
                    prev = act.snap(blk)
                    this = act.snap(prev + 1)
                    act.wait_ge(g_ready, this)
                    act.wait_ge(act_ready, prev)
                    s.activation(sig, gbuf, ACT.Sigmoid, scale=ALPHA).then_inc(sig_ready, 1)
                    gathered(act.snap(prev + 2), this)
                    act.wait_ge(gm_full, this)
                    act.wait_ge(combined, this)
                    s.copy(gm[:].rearrange("p t q -> p (t q)"), turned_g).then_inc(gm_ready, 1)
                    act.wait_ge(aturn_full, this)
                    act.wait_ge(res_full, prev)
                    s.copy(actT, bank_l).then_inc(actT_ready, 1)
                    act.wait_ge(res_full, this)
                    act.wait_ge(combined, this)
                    s.copy(y_sb, bank_y).then_inc(res_ready, 1)
                    act.reg_add(blk, blk, 1)
            total = act.snap(blk)
            act.wait_ge(combined, total + 1)
            act.wait_ge(reloaded, 16)
            for m in range(TT):
                s.activation(fsq_scratch[:, m, :].rearrange("p (q n) -> p q n", q=NQ),
                             sums[:, :, m, :], ACT.Square,
                             accum_out=sumsq_f[:, m:m + 1]).then_inc(fsq_ready, 1)
            root(6, rstd_f)

        @block.vector
        def _(dve):
            v = nc.vector
            steps = [0]

            def link(ins):
                steps[0] += 1
                ins.then_inc(dve_step, 1)
                dve.wait_ge(dve_step, steps[0])

            roots = [0]

            def rstd_of(dst, sq, n):
                link(v.tensor_scalar(dst, sq, 1.0 / n, EPS, ALU.mult, ALU.add))
                v.reciprocal(dst, dst).then_inc(root_in, 1)
                roots[0] += 1
                dve.wait_ge(root_out, roots[0])

            dve.wait_ge(sq_ready, TT)
            rstd_of(rstd, sumsq, D)
            for m in range(TT):
                v.tensor_scalar(xn[:, m, :], x_sb[:, m, :], rstd[:, m:m + 1], None,
                                ALU.mult).then_inc(xn_ready, 1)
            dve.wait_ge(csig_ready, 1)
            v.tensor_tensor(cact, vecT[:, V_C:V_C + KT], csig, ALU.mult).then_inc(cact_ready, 1)
            dve.wait_ge(mod_full, 2)
            dve.wait_ge(bmod_in, 16 * 4)
            v.tensor_tensor(mod_early, mod_early, mod_ps, ALU.add).then_inc(mod_evac, 1)
            dve.wait_ge(mod_ready, 1)
            v.scalar_tensor_tensor(out=A1, in0=modT[:, 8:16], scalar=1.0,
                                   in1=vecT[:, V_GPREMIX:V_GPREMIX + KT],
                                   op0=ALU.add, op1=ALU.mult).then_inc(mod_ready, 1)
            dve.wait_ge(mod_ready, 2)
            dve.wait_ge(xnT_full, 1)
            for k in range(KT // 2):
                last = v.tensor_scalar(hT[:, k, :], bigf[:, k * SEQ:(k + 1) * SEQ], A1[:, k:k + 1],
                                       modT[:, k:k + 1], ALU.mult, ALU.add)
            last.then_inc(hT_dve, 1)
            dve.wait_ge(cols_in, 16 * 12)
            link(v.tensor_scalar(sink8, sink8, 8.0, None, ALU.mult))
            dve.wait_ge(z_evac, 9)
            v.tensor_tensor(v_tok, v_tok, bias_v.unsqueeze(1).to_broadcast([P, TT, P]),
                            ALU.add).then_inc(v_ready, 1)

            def logits(b, L, src, dist_b):
                dve.wait_ge(scores_full, b + 1)
                for h in range(HEADS):
                    slope = 2.0 ** (-8.0 * (h + 1) / HEADS)
                    last = v.scalar_tensor_tensor(out=L[:, h, :], in0=dist_b, scalar=-8.0 * slope,
                                                  in1=src[:, (h % 2) * 4 + h // 2, :], op0=ALU.mult, op1=ALU.add)
                last.then_inc(logits_ready, 1)
                dve.wait_ge(logits_ready, b + 1)
                link(v.tensor_reduce(mx[:, b, :], L, AX.X, ALU.max))
                link(v.tensor_tensor(mx[:, b, :], mx[:, b, :], sink8, ALU.max))
                v.tensor_scalar(negm[:, b, :], mx[:, b, :], -0.125, None,
                                ALU.mult).then_inc(negm_ready, 1)
                dve.wait_ge(negm_ready, 2 * b + 1)
                v.scalar_tensor_tensor(out=sinkp[:, b, :], in0=sink8, scalar=0.125,
                                       in1=negm[:, b, :], op0=ALU.mult,
                                       op1=ALU.add).then_inc(negm_ready, 1)

            def probs(b, L, width):
                dve.wait_ge(probs_exp, b + 1)
                dve.wait_ge(sink_exp, b + 1)
                link(v.tensor_tensor(den[:, b, :], den[:, b, :], sinkp[:, b, :], ALU.add))
                link(v.reciprocal(den[:, b, :], den[:, b, :]))
                v.tensor_tensor(L, L, den[:, b, :].unsqueeze(2).to_broadcast([P, HEADS, width]),
                                ALU.mult).then_inc(probs_ready, 1)

            dve.wait_ge(consts_ready, 2)
            logits(0, L1, bigf.rearrange("p (h k) -> p h k", h=HEADS), dist)
            dve.wait_ge(z_evac, 15)
            for m in range(TT):
                v.tensor_tensor(v_sg[:, m, :], v_sg[:, m, :], bias_vsg,
                                ALU.add).then_inc(vsg_biased, 1)
            logits(1, L0, bigf[:, 0:1024].rearrange("p (h k) -> p h k", h=HEADS), dist[:, P:2 * P])
            for m in range(TT):
                dve.wait_ge(vsg_gelu, m + 1)
                link(v.bn_stats(stats[:, m, :], v_sg[:, m, :]))
                link(v.bn_aggr(mv[:, m, :], stats[:, m, :]))
            rstd_of(ln_rstd, mv[:, :, 1], 1)
            for m in range(TT):
                link(v.tensor_scalar(v_sg[:, m, :], v_sg[:, m, :], mv[:, m, 0:1],
                                     ln_rstd[:, m:m + 1], ALU.subtract, ALU.mult))
                link(v.tensor_tensor(v_sg[:, m, :], v_sg[:, m, :], ln_g, ALU.mult))
                v.tensor_tensor(v_sg[:, m, :], v_sg[:, m, :], ln_b, ALU.add).then_inc(vsg_ready, 1)
            probs(0, L1, 2 * P)
            probs(1, L0, P)

            dve.wait_ge(mix_full, 1)
            link(v.tensor_tensor(
                ysgT.rearrange("p j (b q) -> p j b q", b=2),
                bigf[:, 0:1024].rearrange("p (j b q) -> p j b q", j=4, b=2),
                sg_bias.unsqueeze(2).to_broadcast([P, 4, 2, P]), ALU.add))
            v.tensor_tensor(ysgT, ysgT, uT, ALU.mult).then_inc(ysg_ready, 1)

            dve.wait_ge(late_in, 16 * 14)
            lo, hi = slice(0, P // 2), slice(P // 2, P)
            dve.wait_ge(mod_full, 4)
            link(v.tensor_tensor(mod_late[:, 0, :], mod_late[:, 0, :], mod_ps, ALU.add))
            dve.sem_inc(mod_evac, 1)
            v.tensor_tensor(mod_late[lo, 0, :], mod_late[lo, 0, :], post_rows[lo, 0, :],
                            ALU.mult).then_inc(mod_rows_ready, 1)
            dve.wait_ge(mod_full, 6)
            link(v.tensor_tensor(mod_late[:, 1, :], mod_late[:, 1, :], mod_ps, ALU.add))
            v.scalar_tensor_tensor(out=mod_late[lo, 1, :], in0=mod_late[lo, 1, :], scalar=1.0,
                                   in1=post_rows[lo, 1, :], op0=ALU.add, op1=ALU.mult)
            v.tensor_tensor(mod_late[hi, 1, :], mod_late[hi, 1, :], post_rows[hi, 1, :],
                            ALU.mult).then_inc(mod_rows_ready, 1)

            for n in range(KT):
                dve.wait_ge(br_full, n + 1)
                if n:
                    dve.wait_ge(merged_ready, n)
                src = banks[:, n % 3, :]
                v.tensor_tensor(mT[:, n, :], src[:, 0:SEQ], gate_sig[:, n, :],
                                ALU.mult).then_inc(dve_step, 1)
                v.tensor_tensor(branch, src[:, SEQ:2 * SEQ], gate_sig[:, 8 + n, :],
                                ALU.mult).then_inc(dve_step, 1)
                steps[0] += 2
                dve.wait_ge(dve_step, steps[0])
                v.tensor_tensor(mT[:, n, :], mT[:, n, :], branch, ALU.add).then_inc(merged_ready, 1)

            dve.wait_ge(rowb_evac, 4)
            for m in range(TT):
                one = slice(m, m + 1)
                for h in range(2):
                    dve.wait_ge(y_full, 2 * m + h + 1)
                    c = slice(h * 512, (h + 1) * 512)
                    v.tensor_tensor(xn[:, m, c], y_ps[:, m, c], bias_out[:, c],
                                    ALU.add).then_inc(y_biased, 1)
                dve.wait_ge(ysq_ready, m + 1)
                rstd_of(rstd_y[:, one], sumsq_y[:, one], D)
                link(v.scalar_tensor_tensor(out=xn[:, m, :], in0=xn[:, m, :],
                                            scalar=rstd_y[:, one], in1=rows[:, 0, :],
                                            op0=ALU.mult, op1=ALU.mult))
                v.tensor_tensor(x_sb[:, m, :], x_sb[:, m, :], xn[:, m, :],
                                ALU.add).then_inc(x1_ready, 1)
                dve.wait_ge(x1sq_ready, m + 1)
                rstd_of(rstd_x1[:, one], sumsq_x1[:, one], D)
                link(v.scalar_tensor_tensor(out=h2[:, m, :], in0=x_sb[:, m, :],
                                            scalar=rstd_x1[:, one], in1=rows[:, 1, :],
                                            op0=ALU.mult, op1=ALU.mult))
                v.tensor_tensor(h2[:, m, :], h2[:, m, :], rows[:, 2, :],
                                ALU.add).then_inc(h2_ready, 1)

            dve.wait_ge(logits_full, 1)
            v.tensor_tensor(lg, banks[:, 1, 0:TT * EXPERTS].rearrange("p (t e) -> p t e", t=TT),
                            bias_router.unsqueeze(1).to_broadcast([P, TT, EXPERTS]),
                            ALU.add).then_inc(lg_ready, 1)
            dve.wait_ge(lg_ready, 1)
            dve.sem_inc(front_done, 1)
            link(v.tensor_copy(work, lg))
            wide = [P, TT, EXPERTS]
            for r in range(TOP_K):
                link(v.tensor_reduce(top, work, AX.X, ALU.max))
                if r == 0:
                    v.tensor_scalar(negtop, top, -1.0, None, ALU.mult).then_inc(negtop_ready, 1)
                link(v.tensor_tensor(picked, work, top.unsqueeze(2).to_broadcast(wide),
                                     ALU.is_equal))
                link(v.tensor_tensor(picked, picked, revidx.unsqueeze(1).to_broadcast(wide),
                                     ALU.mult))
                link(v.tensor_reduce(rank, picked, AX.X, ALU.max))
                link(v.tensor_tensor(picked, revidx.unsqueeze(1).to_broadcast(wide),
                                     rank.unsqueeze(2).to_broadcast(wide), ALU.is_equal))
                if r == 0:
                    link(v.tensor_copy(chosen, picked))
                else:
                    link(v.tensor_tensor(chosen, chosen, picked, ALU.add))
                if r < TOP_K - 1:
                    link(v.scalar_tensor_tensor(out=work, in0=picked, scalar=MASKED, in1=work,
                                                op0=ALU.mult, op1=ALU.add))
            dve.sem_inc(chosen_ready, 1)
            dve.wait_ge(gexp_ready, 1)
            link(v.tensor_tensor(gates[:], gates[:], chosen, ALU.mult))
            link(v.tensor_reduce(gsum, gates[:], AX.X, ALU.add))
            link(v.reciprocal(gsum, gsum))
            v.tensor_tensor(gates[:], gates[:], gsum.unsqueeze(2).to_broadcast(wide),
                            ALU.mult).then_inc(gates_ready, 1)
            dve.wait_ge(pos_full, 1)
            pos_ps = banks[:, 2, 0:3 * EXPERTS].rearrange("p (t e) -> p t e", t=3)
            link(v.tensor_scalar(posx[:], pos_ps[:, 0:TT, :], UNROUTED, None, ALU.add))
            link(v.scalar_tensor_tensor(out=posx[:], in0=chosen, scalar=-UNROUTED, in1=posx[:],
                                        op0=ALU.mult, op1=ALU.add))
            link(v.tensor_scalar(blocks_f, pos_ps[:, 2, :], BLK + 0.5, 1.0, ALU.is_gt, ALU.add))
            for j in range(2, MAX_BLOCKS):
                link(v.scalar_tensor_tensor(out=blocks_f, in0=pos_ps[:, 2, :],
                                            scalar=BLK * j + 0.5, in1=blocks_f,
                                            op0=ALU.is_gt, op1=ALU.add))
            v.tensor_copy(nblk[:], blocks_f).then_inc(table_ready, 1)

            dve.wait_ge(b2_used, 1)
            v.memset(y_sb, 0.0).then_inc(res_ready, 1)
            v.memset(gm[:], 0.0).then_inc(gm_ready, 1)
            for done in (g_ready, l_ready, gl_ready, act_ready):
                dve.sem_inc(done, 1)
            dve.wait_ge(table_ready, 1)
            blk = dve.alloc_register("dve_block")
            dve.reg_mov(blk, 1)
            with dve.Fori(0, EXPERTS) as e:
                n = dve.value_load(nblk[0:1, bass.ds(e, 1)], min_val=1, max_val=MAX_BLOCKS)
                with dve.Fori(0, n) as _c:
                    prev = dve.snap(blk)
                    this = dve.snap(prev + 1)
                    dve.wait_ge(g_full, this)
                    v.tensor_scalar(gbuf, bank_g, LIMIT, None, ALU.min).then_inc(g_ready, 1)
                    dve.wait_ge(l_full, this)
                    dve.wait_ge(act_ready, prev)
                    v.tensor_scalar(lbuf, bank_l, LIMIT, -LIMIT, ALU.min,
                                    ALU.max).then_inc(l_ready, 1)
                    dve.wait_ge(l_ready, this)
                    dve.wait_ge(g_ready, this)
                    v.scalar_tensor_tensor(out=lbuf, in0=lbuf, scalar=1.0, in1=gbuf, op0=ALU.add,
                                           op1=ALU.mult).then_inc(gl_ready, 1)
                    dve.wait_ge(gl_ready, this)
                    dve.wait_ge(sig_ready, this)
                    v.tensor_tensor(lbuf, lbuf, sig, ALU.mult).then_inc(act_ready, 1)
                    dve.reg_add(blk, blk, 1)
            dve.wait_ge(fsq_ready, TT)
            rstd_of(rstd_f, sumsq_f, D)
            dve.wait_ge(reloaded, 16)
            for m in range(TT):
                link(v.scalar_tensor_tensor(
                    out=y_out[:, m, :].rearrange("p (q n) -> p q n", q=NQ), in0=sums[:, :, m, :],
                    scalar=rstd_f[:, m:m + 1], in1=row_back.rearrange("p (q n) -> p q n", q=NQ),
                    op0=ALU.mult, op1=ALU.mult))
                v.tensor_tensor(y_out[:, m, :], y_out[:, m, :], x1_back[:, m, :],
                                ALU.add).then_inc(out_ready, 1)

        @block.tensor
        def _(pe):
            mm, tr = nc.tensor.matmul, nc.tensor.transpose

            def piece_in(n):
                pe.wait_ge(slot_full[n % FRONT_SLOTS], 16 * (n // FRONT_SLOTS + 1))
                return W[:, n % FRONT_SLOTS]

            pe.wait_ge(consts_ready, 1)
            pe.wait_ge(vecs_in, 16 * 6)
            tr(banks[:, 0, 0:V_ROWS], vec_rows[0:V_ROWS, :],
               ident[0:V_ROWS, 0:V_ROWS]).then_inc(z_full, 1)
            pe.wait_ge(sgw_in, 16)
            for half in range(2):
                for g in range(4):
                    last = tr(banks[:, 1 + half, g * P:(g + 1) * P],
                              sg_rows[:, 4 * half + g, :], ident[:])
                last.then_inc(z_full, 1)
            pe.wait_ge(xn_ready, TT)
            for k in range(KT):
                for m in range(TT):
                    last = tr(bigf[:, k * SEQ + m * P:k * SEQ + (m + 1) * P],
                              xn[:, m, k * P:(k + 1) * P], ident[:])
            last.then_inc(xnT_full, 1)

            def modulation(i, n):
                w = piece_in(n)
                for k in range(KT):
                    for h in range(2):
                        at = (2 * (i % 2) + h) * QUARTER
                        last = mm(mod_ps[at:at + QUARTER, :],
                                  cact[:, k:k + 1].to_broadcast([P, QUARTER]),
                                  w[:, k, h * HALF:(h + 1) * HALF], start=(k == 0),
                                  stop=(k == KT - 1))
                last.then_inc(mod_full, 1)

            pe.wait_ge(cact_ready, 1)
            for n in MOD_EARLY:
                modulation(n, n)
            pe.wait_ge(mod_evac, 1)
            for j in range(4):
                last = tr(mod_ps[:, j * P:(j + 1) * P], mod_early[:, j * P:(j + 1) * P], ident[:])
            last.then_inc(modT_full, 1)

            pe.wait_ge(hT_dve, 1)
            pe.wait_ge(hT_act, 1)

            def z_bank(r):
                pe.wait_ge(z_evac, r - 2)
                return banks[:, r % 3, :]

            def z_transposed(r, w, cols):
                b = z_bank(r)
                for k in range(KT):
                    last = mm(b[:, 0:SEQ], w[:, k, cols], hT[:, k, :], start=(k == 0),
                              stop=(k == KT - 1))
                last.then_inc(z_full, 1)

            w = piece_in(IN_PIECES[0])
            for j in range(4):
                z_transposed(3 + j, w, slice(j * P, (j + 1) * P))
            z_transposed(7, w, slice(512, 640))
            b = z_bank(8)
            for m in range(TT):
                for k in range(KT):
                    last = mm(b[:, m * P:(m + 1) * P], hT[:, k, m * P:(m + 1) * P],
                              w[:, k, 640:768], start=(k == 0), stop=(k == KT - 1))
            last.then_inc(z_full, 1)
            for j in range(2):
                z_transposed(9 + j, w, slice(768 + j * P, 768 + (j + 1) * P))

            def scores(b, width):
                pe.wait_ge(z_evac, 8)
                pe.wait_ge(k_swapped, 1)
                q = slice(P, 2 * P) if b == 0 else slice(0, P)
                for h in range(HEADS):
                    part = slice((h % 2) * HD, (h % 2 + 1) * HD)
                    keys = kT if h % 2 == h // 4 else kT_swapped
                    at = ((h % 2) * 4 + h // 2) * width
                    last = mm(bigf[:, at:at + width], qT[part, h // 2, q],
                              keys[part, 0:width], start=True, stop=True)
                last.then_inc(scores_full, 1)

            scores(0, 2 * P)
            w = piece_in(IN_PIECES[1])
            for j in range(2):
                z_transposed(11 + j, w, slice(j * P, (j + 1) * P))
            for m in range(TT):
                b = z_bank(13 + m)
                for k in range(KT):
                    last = mm(b, hT[:, k, m * P:(m + 1) * P], w[:, k, 256:768], start=(k == 0),
                              stop=(k == KT - 1))
                last.then_inc(z_full, 1)
            for j in range(2):
                z_transposed(15 + j, w, slice(768 + j * P, 768 + (j + 1) * P))
            pe.wait_ge(logits_ready, 1)
            scores(1, P)
            w = piece_in(IN_PIECES[2])
            for j in range(8):
                z_transposed(17 + j, w, slice(j * P, (j + 1) * P))
            w = piece_in(IN_PIECES[3])
            for j in range(6):
                z_transposed(25 + j, w, slice(j * P, (j + 1) * P))

            pe.wait_ge(probs_ready, 2)
            tiles = [L0[:, h, :] for h in range(HEADS)] + [
                L1[:, h, kb * P:(kb + 1) * P] for h in range(HEADS) for kb in range(2)]
            for r in range(3):
                if r == 0:
                    pe.wait_ge(logits_ready, 2)
                if r == 2:
                    pe.wait_ge(pT_evac, 1)
                b = 1024 * (r % 2)
                for i in range(8):
                    last = tr(bigf[:, b + i * P:b + (i + 1) * P], tiles[8 * r + i], ident[:])
                last.then_inc(pT_full, 1)
                if r == 1:
                    pe.wait_ge(mod_ready, 1)
                    modulation(2, MOD_LATE[0])
            modulation(3, MOD_LATE[1])
            pe.wait_ge(v_ready, 1)
            pe.wait_ge(pT_evac, 3)
            for h in range(HEADS):
                vh = slice((h // 4) * HD, (h // 4 + 1) * HD)
                rows_h = slice((h % 2) * HD, (h % 2 + 1) * HD)
                at = 1024 + (h // 2) * SEQ
                mm(bigf[rows_h, at:at + P], v_tok[:, 0, vh], pT[:, h, :], start=True, stop=True)
                for kb in range(2):
                    last = mm(bigf[rows_h, at + P:at + 2 * P], v_tok[:, kb, vh],
                              pT[:, 8 + 2 * h + kb, :], start=(kb == 0), stop=(kb == 1))
            last.then_inc(att_full, 1)
            pe.wait_ge(vsg_ready, TT)
            pe.wait_ge(masked_w, 1)
            for g in range(GROUPS):
                rows_g = slice((g % 2) * HD, (g % 2 + 1) * HD)
                for m in range(TT):
                    at = (g // 2) * SEQ + m * P
                    last = mm(bigf[rows_g, at:at + P], v_sg[:, m, g * HD:(g + 1) * HD], wT[:, g, :],
                              start=True, stop=True)
            last.then_inc(mix_full, 1)
            pe.wait_ge(mod_evac, 2)
            modulation(4, MOD_LATE[2])
            modulation(5, MOD_LATE[3])

            pe.wait_ge(att_evac, 1)
            pe.wait_ge(ysg_ready, 1)
            for i in range(2):
                pe.wait_ge(mod_rows_ready, i + 1)
                if i:
                    pe.wait_ge(rowb_evac, 2)
                for r in range(4):
                    q = slice(r * QUARTER, r * QUARTER + 1)
                    last = mm(big[:, r, :], ones[q, :], mod_late[q, i, :], start=True, stop=True)
                last.then_inc(rowb_full, 1)

            w = piece_in(BR_PIECE)
            pe.wait_ge(br_sg_full, 16)
            pe.wait_ge(z_evac, 31)
            for n in range(KT):
                if n >= 3:
                    pe.wait_ge(merged_ready, n - 2)
                for side, src in ((0, yattT), (1, ysgT)):
                    for k in range(4):
                        last = mm(banks[:, n % 3, side * SEQ:(side + 1) * SEQ],
                                  w[:, 4 * side + k, n * P:(n + 1) * P], src[:, k, :],
                                  start=(k == 0), stop=(k == 3))
                last.then_inc(br_full, 1)
            w = piece_in(OUT_PIECE)
            pe.wait_ge(merged_ready, KT)
            pe.wait_ge(rowb_evac, 4)
            for m in range(TT):
                for h in range(2):
                    c = slice(h * 512, (h + 1) * 512)
                    for k in range(KT):
                        last = mm(y_ps[:, m, c], mT[:, k, m * P:(m + 1) * P], w[:, k, c],
                                  start=(k == 0), stop=(k == KT - 1))
                    last.then_inc(y_full, 1)

            for m in range(TT):
                if m == 0:
                    pe.wait_ge(y_biased, 2 * TT)
                pe.wait_ge(h2_ready, m + 1)
                for k in range(KT):
                    last = tr(bigf[:, k * SEQ + m * P:k * SEQ + (m + 1) * P],
                              h2[:, m, k * P:(k + 1) * P], ident[:])
            last.then_inc(h2T_full, 1)
            pe.wait_ge(h2T_evac, 1)
            for k in range(KT):
                last = mm(banks[0:EXPERTS, 0, 0:SEQ], wr[:, k, :], hT[:, k, :], start=(k == 0),
                          stop=(k == KT - 1))
            last.then_inc(lgT_full, 1)
            pe.wait_ge(lgT_ready, 1)
            for m in range(TT):
                last = tr(banks[:, 1, m * EXPERTS:(m + 1) * EXPERTS], lgT[:, m * P:(m + 1) * P],
                          ident[0:EXPERTS, 0:EXPERTS])
            last.then_inc(logits_full, 1)
            pe.wait_ge(chosen_ready, 1)
            pe.wait_ge(consts_ready, 5)
            E = EXPERTS
            mm(banks[:, 2, 0:E], U, chosen[:, 0, :], start=True, stop=True)
            mm(banks[:, 2, E:2 * E], ones, chosen[:, 0, :], start=True, stop=False)
            mm(banks[:, 2, E:2 * E], U, chosen[:, 1, :], start=False, stop=True)
            mm(banks[:, 2, 2 * E:3 * E], ones, chosen[:, 0, :], start=True, stop=False)
            mm(banks[:, 2, 2 * E:3 * E], ones, chosen[:, 1, :], start=False,
               stop=True).then_inc(pos_full, 1)
            pe.wait_ge(gates_ready, 1)
            for m in range(TT):
                last = tr(banks[0:E, 3, m * P:(m + 1) * P], gates[:, m, :], ident[:])
            last.then_inc(gT_full, 1)
            pe.wait_ge(gT_ready, 1)
            for q in range(NQ):
                for m in range(TT):
                    last = mm(sums[:, q, m, :], gT[:, m, :], b2_sb[:, q * QW:(q + 1) * QW],
                              start=(m == 0), stop=False, skip_group_check=True)
            last.then_inc(b2_used, 1)

            for done in (xturn_full, gm_full, g_full, l_full, aturn_full, res_full, combined,
                         gather_full):
                pe.sem_inc(done, 1)
            pe.wait_ge(table_ready, 1)
            blk = pe.alloc_register("pe_block")
            pe.reg_mov(blk, 1)
            part = [slice(q * BLK, (q + 1) * BLK) for q in range(NQ)]
            cols = [slice(q * QW, (q + 1) * QW) for q in range(NQ)]

            def gather():
                for m in range(TT):
                    for q in range(NQ):
                        last = mm(bank_x[part[q], :], sel[:, m, :], h2[:, m, cols[q]],
                                  start=(m == 0), stop=(m == TT - 1))
                last.then_inc(gather_full, 1)

            def combine(stop):
                for m in range(TT):
                    for q in range(NQ):
                        last = mm(sums[:, q, m, :], gm[part[q], m, :], y_sb[part[q], :],
                                  start=False, stop=stop, skip_group_check=True)
                last.then_inc(combined, 1)

            def turn(bank, rows_sb, full):
                for j in range(2):
                    last = tr(bank[:, j * P:(j + 1) * P], rows_sb[:, j * P:(j + 1) * P], ident[:])
                last.then_inc(full, 1)

            def layer(bank, w, turned, bias_row, full):
                if bias_row is not None:
                    for q in range(NQ):
                        mm(bank[part[q], :], bsel[:, bias_row + q // 2, :],
                           b1q[:, (q % 2) * QW:(q % 2 + 1) * QW], start=True, stop=False)
                for k in range(KT):
                    at = (k % 2) * P + (k // 2) * BLK
                    for q in range(NQ):
                        last = mm(bank[part[q], :], turned[:, at:at + BLK], w[:, k, cols[q]],
                                  start=(bias_row is None and k == 0), stop=(k == KT - 1))
                last.then_inc(full, 1)

            def expert_block(base, full):
                prev = pe.snap(blk)
                this = pe.snap(prev + 1)
                following = pe.snap(prev + 2)
                pe.wait_ge(gm_ready, prev)
                pe.wait_ge(bsel_ready, this)
                pe.wait_ge(xgT_ready, this)
                pe.wait_ge(slot_full[base], full)
                layer(bank_g, W[:, base], xgT, 0, g_full)
                pe.wait_ge(sel_ready, following)
                gather()
                pe.wait_ge(actT_ready, prev)
                pe.wait_ge(slot_full[base + 1], full)
                layer(bank_l, W[:, base + 1], xgT, 2, l_full)
                pe.wait_ge(res_ready, prev)
                combine(False)
                pe.wait_ge(xg_evac, following)
                turn(bank_y, xg_rows, xturn_full)
                pe.wait_ge(g_ready, this)
                pe.wait_ge(gsel_ready, this)
                for m in range(TT):
                    last = tr(turned_g[:, m * P:(m + 1) * P],
                              gsel[:, m].rearrange("p a s -> p (a s)"), ident[:])
                last.then_inc(gm_full, 1)
                pe.wait_ge(act_ready, this)
                turn(bank_l, lbuf, aturn_full)
                pe.wait_ge(actT_ready, this)
                pe.wait_ge(xgT_ready, following)
                pe.wait_ge(slot_full[base + 2], full)
                layer(bank_y, W[:, base + 2], actT, None, res_full)
                pe.reg_add(blk, blk, 1)

            pe.wait_ge(sel_ready, 2)
            gather()
            pe.wait_ge(xg_evac, 2)
            turn(bank_y, xg_rows, xturn_full)
            with pe.Fori(0, EXPERTS // 2) as i:
                for half in range(2):
                    n = pe.value_load(nblk[0:1, bass.ds(2 * i + half, 1)], min_val=1,
                                      max_val=MAX_BLOCKS)
                    first = FRONT_PIECES // FRONT_SLOTS + 1 if half == 0 else 1
                    full = pe.snap(16 * i + 16 * first)
                    with pe.Fori(0, n) as _c:
                        expert_block(3 * half, full)
            total = pe.snap(blk)
            pe.wait_ge(gm_ready, total)
            pe.wait_ge(res_ready, total)
            combine(True)


_INS = ["x", "c", "w_mod", "b_mod", "g_pre_mix", "g_post_mix", "w_in", "b_in", "attn_sinks",
        "sg_ln_g", "sg_ln_b", "sg_w", "sg_b", "w_br_attn", "w_br_sg", "w_out", "b_out",
        "g_pre_ffn", "g_post_ffn", "w_router", "b_router", "w_mlp1", "b_mlp1", "w_mlp2", "b_mlp2"]


def kernel(**inputs):
    import concourse.bacc as bacc
    from concourse.bass_utils import run_bass_kernel_spmd

    nc = bacc.Bacc("TRN2", target_bir_lowering=False, num_devices=1, dynamic_dma_scratch_size=64)
    arrays, t = {}, {}
    for name in _INS:
        a = np.ascontiguousarray(inputs[name])
        arrays[name] = a
        t[name] = nc.dram_tensor(name, a.shape, F32, kind="ExternalInput").ap()
    out = nc.dram_tensor("out", (1, SEQ, D), F32, kind="ExternalOutput").ap()
    layer_program(nc, t, out)
    r = run_bass_kernel_spmd(nc, [arrays], core_ids=[0])
    return r.results[0]["out"]
```

```python
from contextlib import ExitStack

import numpy as np

import concourse.bass as bass
import concourse.mybir as mybir

F32 = mybir.dt.float32
I32 = mybir.dt.int32
ACT = mybir.ActivationFunctionType
ALU = mybir.AluOpType
AX = mybir.AxisListType

P = 128
SEQ, D = 256, 1024
TT = SEQ // P
KT = D // P
HEADS, HD = 8, 64
GROUPS, SGW = 8, 512
EXPERTS, TOP_K = 32, 4
BLK = 32
MAX_BLOCKS = SEQ // BLK
HALF = 512
NQ, QW = 4, D // 4
QUARTER = 32
ALPHA, LIMIT, EPS = 1.702, 7.0, 1e-6
SLOTS, PIECE = 6, KT * D
FRONT_SLOTS = 3
FAR = 1.0e30
MASKED = -1.0e30
UNROUTED = 10000.0

MOD_EARLY, IN_PIECES, MOD_LATE = [0, 1], [2, 3, 5, 7], [4, 6, 8, 9]
BR_PIECE, OUT_PIECE, FRONT_PIECES = 10, 11, 12

V_C, V_GPREMIX, V_BQ, V_BK, V_BU, V_BG, V_ROWS = 0, 8, 16, 20, 21, 25, 41

RANKS = EXPERTS - 2
FULLER = RANKS // 2 - 1
FULL_RANKS = [(5 * k + 12) % FULLER for k in range(FULLER)]
EMPTY_RANKS = list(range(RANKS - 1, FULLER - 1, -1))
RANK_OF_TURN = ([EMPTY_RANKS[0]] + [r for pair in zip(FULL_RANKS, EMPTY_RANKS[1:]) for r in pair]
                + [EMPTY_RANKS[-1]])


def layer_program(nc, t, out):
    ctx = ExitStack()
    with ctx:
        def sb(name, shape, dt=F32):
            return ctx.enter_context(nc.sbuf_tensor(name, shape, dt))

        def sem(name):
            return ctx.enter_context(nc.semaphore(name))

        W = sb("weight_slots", [P, SLOTS, KT, D])
        h2 = sb("h2", [P, TT, D])
        ident = sb("ident", [P, P])
        slot_iota = sb("slot_iota", [P, SEQ])
        b1q = sb("b1q", [P, HALF])
        posx = sb("posx", [P, TT, EXPERTS])
        gates = sb("gates", [P, TT, EXPERTS])
        order = sb("order", [P, EXPERTS], I32)
        nblk = sb("nblk", [P, EXPERTS], I32)
        sel = sb("sel", [P, TT, BLK])
        gsel = sb("gsel", [P, TT, NQ, BLK])
        bsel = sb("bsel", [P, 4, BLK])
        work_sb = sb("work_sb", [P, 7, QW])
        xg_rows, xgT, gbuf, sig, lbuf, actT, y_sb = (work_sb[:, i, :] for i in range(7))
        gm = sb("gm", [P, TT, P])
        mod_late = sb("mod_late", [P, 2, HALF])
        post_rows = sb("post_rows", [P, 2, HALF])
        small = sb("small", [P, 456])

        work_flat = work_sb[:].rearrange("p a b -> p (a b)")
        U, ones = work_flat[:, 0:P], work_flat[:, P:2 * P]
        gT = mod_late[0:EXPERTS, 0, 0:SEQ].rearrange("p (t q) -> p t q", t=TT)
        b2_sb = work_flat[0:EXPERTS, 512:1536]
        wr = work_flat[:, 1536:1792].rearrange("p (k e) -> p k e", k=KT)

        front = W[:, FRONT_SLOTS:SLOTS, :, :].rearrange("p s k n -> p (s k n)")
        place = [0]

        def fb(*dims):
            n = int(np.prod(dims))
            a = front[:, place[0]:place[0] + n]
            place[0] += n
            assert place[0] <= FRONT_SLOTS * PIECE, place[0]
            names = [f"d{i}" for i in range(len(dims))]
            return a if len(dims) == 1 else a.rearrange(
                f"p ({' '.join(names)}) -> p {' '.join(names)}",
                **{n: d for n, d in zip(names, dims)})

        gate_sig = fb(16, SEQ)
        yattT, ysgT = fb(4, SEQ), fb(4, SEQ)
        sg_rows = front[:, 4096:4096 + GROUPS * P].rearrange("p (g s) -> p g s", g=GROUPS)
        L0 = fb(HEADS, P)
        ln_g, ln_b = fb(SGW), fb(SGW)
        assert place[0] == PIECE
        x_sb = fb(TT, D)
        hT = fb(KT, SEQ)
        xn = fb(TT, D)
        at = place[0] - 2 * TT * D
        pT = front[:, at:at + 24 * P].rearrange("p (i q) -> p i q", i=24)
        at = place[0]
        qT = fb(4, SEQ)
        kT, kT_swapped = fb(SEQ), fb(SEQ)
        v_tok = fb(TT, P)
        uT = fb(4, SEQ)
        v_sg = fb(TT, SGW)
        wT = fb(GROUPS, P)
        rows = front[:, at:at + 4 * D].rearrange("p (r n) -> p r n", r=4)
        L1 = fb(HEADS, 2 * P)
        at = place[0] - KT * SEQ
        mT = front[:, at:at + KT * SEQ].rearrange("p (k s) -> p k s", k=KT)
        mod_early = front[:, at:at + HALF]
        dist = fb(2 * P)
        bias_vsg = fb(SGW)
        bias_v = fb(P)
        bias_out = fb(D)
        sg_bias = fb(4, P)
        vec_rows = fb(P)
        vecT = fb(P)
        modT = fb(16)
        branch = fb(SEQ)
        f_small = fb(320)

        fs = [0]

        def fcols(n):
            fs[0] += n
            assert fs[0] <= 320
            return f_small[:, fs[0] - n:fs[0]]

        sumsq, rstd = fcols(TT), fcols(TT)
        sumsq_y, rstd_y = fcols(2 * TT), fcols(TT)
        sumsq_x1, rstd_x1 = fcols(2 * TT), fcols(TT)
        csig, cact = fcols(KT), fcols(KT)
        A1 = fcols(KT)
        sink8 = fcols(HEADS)
        mx = fcols(2 * HEADS).rearrange("p (b h) -> p b h", b=2)
        negm = fcols(2 * HEADS).rearrange("p (b h) -> p b h", b=2)
        den = fcols(2 * HEADS).rearrange("p (b h) -> p b h", b=2)
        sinkp = fcols(2 * HEADS).rearrange("p (b h) -> p b h", b=2)
        stats = fcols(TT * 6).rearrange("p (t c) -> p t c", t=TT)
        mv = fcols(TT * 2).rearrange("p (t c) -> p t c", t=TT)
        ln_rstd = fcols(TT)

        sm = [0]

        def scols(*dims):
            n = int(np.prod(dims))
            sm[0] += n
            assert sm[0] <= 456
            a = small[:, sm[0] - n:sm[0]]
            return a if len(dims) == 1 else a.rearrange("p (a b) -> p a b", a=dims[0])

        bias_router = scols(EXPERTS)
        revidx = scols(EXPERTS)
        padded = scols(TT, EXPERTS + TOP_K)
        largest = scols(TT, 2 * TOP_K)
        chosen = scols(TT, EXPERTS)
        negtop, gsum = scols(TT), scols(TT)
        blocks_f, ends = scols(EXPERTS), scols(MAX_BLOCKS - 1)
        warm = scols(1)
        key, rank, turn_rank = scols(RANKS), scols(RANKS), scols(RANKS)
        sumsq_f, rstd_f = scols(TT), scols(TT)

        banks = ctx.enter_context(nc.psum_tensor("banks", [P, 8, 512], F32))
        big = banks[:, 4:8, :]
        bigf = big.rearrange("p b n -> p (b n)")
        mod_ps = banks[:, 3, :]
        bank_g, bank_l, bank_y, bank_x = (banks[:, b, 0:QW] for b in range(4))
        turned_g = bank_g
        y_ps = bigf.rearrange("p (t n) -> p t n", t=TT)
        h2T_ps = bigf.rearrange("p (t k q) -> p t k q", t=TT, k=KT)
        sums = big.rearrange("p q (t n) -> p q t n", t=TT)

        park = nc.dram_tensor("parked", (P, (TT + 1) * D), F32).ap()

        slot_full = [sem(f"slot_full_{s}") for s in range(SLOTS)]
        br_sg_full = sem("br_sg_full")
        w2_rest_full = [sem("w2_rest_full_even"), sem("w2_rest_full_odd")]
        distance_ready = sem("distance_ready")
        early_issued, early_may_go, rest_may_go = map(sem, (
            "early_issued", "early_may_go", "rest_may_go"))
        mod_rest_full = [sem("mod_rest_full_0"), sem("mod_rest_full_1")]
        in_rest_full = sem("in_rest_full")
        x_in, vecs_in, bmod_in, sgw_in, cols_in = map(sem, (
            "x_in", "vecs_in", "bmod_in", "sgw_in", "cols_in"))
        warm_ready = sem("warm_ready")
        consts_ready, masked_w = sem("consts_ready"), sem("masked_w")
        dve_step, act_step, pool_step = sem("dve_step"), sem("act_step"), sem("pool_step")
        sq_ready, xn_ready, xnT_full = sem("sq_ready"), sem("xn_ready"), sem("xnT_full")
        cact_ready, csig_ready = sem("cact_ready"), sem("csig_ready")
        k_swapped = sem("k_swapped")
        root_in, root_out = sem("root_in"), sem("root_out")
        mod_full, mod_ready = sem("mod_full"), sem("mod_ready")
        mod_evac, modT_full, late_in = sem("mod_evac"), sem("modT_full"), sem("late_in")
        hT_dve, hT_act = sem("hT_dve"), sem("hT_act")
        z_full, z_evac = sem("z_full"), sem("z_evac")
        scores_full, logits_ready, probs_exp, probs_ready = map(sem, (
            "scores_full", "logits_ready", "probs_exp", "probs_ready"))
        negm_ready, sink_exp = sem("negm_ready"), sem("sink_exp")
        pT_full, pT_evac = sem("pT_full"), sem("pT_evac")
        att_full, att_evac = sem("att_full"), sem("att_evac")
        vsg_biased, vsg_gelu, vsg_ready, v_ready = map(sem, (
            "vsg_biased", "vsg_gelu", "vsg_ready", "v_ready"))
        mix_full, ysg_ready = sem("mix_full"), sem("ysg_ready")
        mod_rows_ready, rowb_full, rowb_evac = map(sem, (
            "mod_rows_ready", "rowb_full", "rowb_evac"))
        br_full, merged_ready = sem("br_full"), sem("merged_ready")
        y_full, y_biased, ysq_ready = sem("y_full"), sem("y_biased"), sem("ysq_ready")
        x1_ready, x1sq_ready, h2_ready = sem("x1_ready"), sem("x1sq_ready"), sem("h2_ready")
        h2T_full, h2T_evac, h2T_dve = sem("h2T_full"), sem("h2T_evac"), sem("h2T_dve")
        logits_full, lg_ready = sem("logits_full"), sem("lg_ready")
        negtop_ready, gexp_ready, chosen_ready = map(sem, (
            "negtop_ready", "gexp_ready", "chosen_ready"))
        pos_full, gates_ready, gT_full, gT_ready = map(sem, (
            "pos_full", "gates_ready", "gT_full", "gT_ready"))
        order_ready, sums_open = sem("order_ready"), sem("sums_open")
        table_ready, front_done, parked = sem("table_ready"), sem("front_done"), sem("parked")
        sel_ready, gsel_ready, bsel_ready, pool_waits, g_ready, l_ready, gl_ready, act_ready = map(
            sem, ("sel_ready", "gsel_ready", "bsel_ready", "pool_waits", "g_ready", "l_ready",
                  "gl_ready", "act_ready"))
        xg_evac, xgT_ready, gm_ready, sig_ready, actT_ready, res_ready = map(sem, (
            "xg_evac", "xgT_ready", "gm_ready", "sig_ready", "actT_ready", "res_ready"))
        gather_full, xturn_full, gm_full, g_full, l_full, aturn_full, res_full, combined = map(
            sem, ("gather_full", "xturn_full", "gm_full", "g_full", "l_full", "aturn_full",
                  "res_full", "combined"))
        reloaded, fsq_ready, normed, first_out_ready, out_ready, out_done = map(sem, (
            "reloaded", "fsq_ready", "normed", "first_out_ready", "out_ready", "out_done"))

        def piece(w):
            return w.rearrange("(k p) n -> p k n", p=P)

        w_mod, w_in = piece(t["w_mod"][0]), piece(t["w_in"][0])
        w_br_attn, w_br_sg = piece(t["w_br_attn"][0]), piece(t["w_br_sg"][0])
        w_out = piece(t["w_out"][0])
        w1 = t["w_mlp1"].rearrange("l e (k p) n -> (l e) p k n", p=P)
        w2 = t["w_mlp2"].rearrange("l e (k p) n -> (l e) p k n", p=P)
        x_dram = t["x"].rearrange("b (t p) n -> p (b t) n", p=P)
        out_dram = out.rearrange("b (t p) n -> p (b t) n", p=P)
        IN_W = t["w_in"].shape[2]

        x1_back = W[:, 0, 0:TT, :]
        row_back = W[:, 0, TT, :]
        y_out = W[:, 1, 0:TT, :]
        fsq_scratch = W[:, 1, TT:2 * TT, :]

        piece_done = [(mod_full, 1), (mod_full, 2), (z_full, 11), (z_full, 17), (mod_full, 3),
                      (z_full, 25), (mod_full, 4), (z_full, 31), (mod_full, 5), (mod_full, 6),
                      (br_full, KT), (y_full, 2 * TT)]

        block = ctx.enter_context(nc.Block())

        @block.sync
        def _(sp):
            for n in range(FRONT_PIECES):
                s = n % FRONT_SLOTS
                if n >= FRONT_SLOTS:
                    sp.wait_ge(*piece_done[n - FRONT_SLOTS])
                if n == 0:
                    sp.wait_ge(early_issued, 1)
                if n == IN_PIECES[0]:
                    sp.sem_inc(early_may_go, 1)
                    sp.wait_ge(early_issued, 2)
                if n in MOD_EARLY:
                    for k, done in ((slice(0, 4), slot_full[s]), (slice(4, 8), mod_rest_full[n])):
                        sp.dma_start(W[:, s, k], w_mod[:, k, n * D:(n + 1) * D]).then_inc(done, 16)
                elif n == IN_PIECES[0]:
                    for h in range(2):
                        sp.dma_start(W[:, s, :, h * HALF:(h + 1) * HALF],
                                     w_in[:, :, h * HALF:(h + 1) * HALF]
                                     ).then_inc((slot_full[s], in_rest_full)[h], 16)
                    sp.sem_inc(rest_may_go, 1)
                elif n in IN_PIECES:
                    a = IN_PIECES.index(n) * D
                    b = min(a + D, IN_W)
                    sp.dma_start(W[:, s, :, 0:b - a], w_in[:, :, a:b]).then_inc(slot_full[s], 16)
                elif n in MOD_LATE:
                    a = (MOD_LATE.index(n) + 2) * D
                    sp.dma_start(W[:, s], w_mod[:, :, a:a + D]).then_inc(slot_full[s], 16)
                elif n == BR_PIECE:
                    sp.dma_start(W[:, s, 0:4], w_br_attn).then_inc(slot_full[s], 16)
                    sp.dma_start(W[:, s, 4:8], w_br_sg).then_inc(br_sg_full, 16)
                else:
                    sp.dma_start(W[:, s], w_out).then_inc(slot_full[s], 16)

            def load_w2(e, half):
                for rows_half, done in ((slice(0, 4), slot_full[3 * half + 2]),
                                        (slice(4, 8), w2_rest_full[half])):
                    sp.dma_start(W[:, 3 * half + 2, rows_half], w2[e, :, rows_half]).then_inc(done, 16)

            def load(e, half, value):
                s = 3 * half
                sp.wait_ge(g_full, value)
                sp.dma_start(W[:, s], w1[e, :, :, 0:D]).then_inc(slot_full[s], 16)
                sp.wait_ge(l_full, value)
                sp.dma_start(W[:, s + 1], w1[e, :, :, D:2 * D]).then_inc(slot_full[s + 1], 16)
                sp.wait_ge(res_full, value)
                load_w2(e, half)

            sp.wait_ge(*piece_done[FRONT_PIECES - 3])
            sp.dma_start(W[:, 0], w1[0, :, :, 0:D]).then_inc(slot_full[0], 16)
            sp.wait_ge(*piece_done[FRONT_PIECES - 2])
            sp.dma_start(W[:, 1], w1[0, :, :, D:2 * D]).then_inc(slot_full[1], 16)
            sp.wait_ge(merged_ready, KT)
            sp.dma_start(W[:, 3], w1[1, :, :, 0:D]).then_inc(slot_full[3], 16)
            sp.wait_ge(*piece_done[FRONT_PIECES - 1])
            load_w2(0, 0)
            sp.wait_ge(x1_ready, 2 * TT)
            sp.dma_start(park[:, 0:TT * D], x_sb.rearrange("p t n -> p (t n)")).then_inc(parked, 16)
            sp.wait_ge(rowb_evac, 4)
            sp.dma_start(park[:, TT * D:(TT + 1) * D], rows[:, 3, :]).then_inc(parked, 16)
            sp.wait_ge(parked, 32)
            sp.wait_ge(front_done, 1)
            sp.dma_start(W[:, 4], w1[1, :, :, D:2 * D]).then_inc(slot_full[4], 16)
            load_w2(1, 1)
            sp.wait_ge(order_ready, 1)
            used = sp.alloc_register("blocks_used")
            sp.reg_mov(used, 1)
            with sp.Fori(1, EXPERTS // 2) as i:
                for half in range(2):
                    n = sp.value_load(nblk[0:1, bass.ds(2 * i - 2 + half, 1)],
                                      min_val=1, max_val=MAX_BLOCKS)
                    e = sp.value_load(order[0:1, bass.ds(2 * i + half, 1)],
                                      min_val=2, max_val=EXPERTS - 1)
                    sp.reg_add(used, used, n)
                    load(e, half, sp.snap(used))
            n = sp.value_load(nblk[0:1, EXPERTS - 2:EXPERTS - 1], min_val=1, max_val=MAX_BLOCKS)
            sp.reg_add(used, used, n)
            sp.wait_ge(g_full, sp.snap(used))
            sp.dma_start(W[:, 0, 0:TT + 1, :].rearrange("p k n -> p (k n)"),
                         park).then_inc(reloaded, 16)
            sp.wait_ge(first_out_ready, 1)
            sp.dma_start(out_dram[:, 0, :], y_out[:, 0, :]).then_inc(out_done, 16)
            for h in range(2):
                c = slice(h * HALF, (h + 1) * HALF)
                sp.wait_ge(out_ready, h + 1)
                sp.dma_start(out_dram[:, 1, c], y_out[:, 1, c]).then_inc(out_done, 16)
            sp.wait_ge(out_done, 16 * 3)

        @block.gpsimd
        def _(pool):
            g = nc.gpsimd
            g.memset(ident[:], 0.0).then_inc(pool_step, 1)
            g.memset(ones, 1.0).then_inc(pool_step, 1)
            pool.wait_ge(pool_step, 2)
            g.affine_select(out=ident[:], in_=ident[:], compare_op=ALU.not_equal, fill=1.0, base=0,
                            pattern=[[-1, P]], channel_multiplier=1).then_inc(consts_ready, 1)
            g.iota(dist, [[-1, 2 * P]], base=P, channel_multiplier=1,
                   allow_small_or_imprecise_dtypes=True).then_inc(pool_step, 1)
            pool.wait_ge(pool_step, 3)
            g.affine_select(out=dist, in_=dist, compare_op=ALU.is_ge, fill=FAR, base=P,
                            pattern=[[-1, 2 * P]], channel_multiplier=1).then_inc(pool_step, 1)
            pool.wait_ge(pool_step, 4)
            g.affine_select(out=dist, in_=dist, compare_op=ALU.is_ge, fill=FAR, base=-1,
                            pattern=[[1, 2 * P]], channel_multiplier=-1).then_inc(consts_ready, 1)
            g.affine_select(out=U, in_=ones, compare_op=ALU.is_ge, fill=0.0, base=-1,
                            pattern=[[1, P]], channel_multiplier=-1).then_inc(consts_ready, 1)
            g.iota(slot_iota[:], [[1, SEQ]], base=0, channel_multiplier=0,
                   allow_small_or_imprecise_dtypes=True).then_inc(consts_ready, 1)
            g.iota(revidx, [[-1, EXPERTS]], base=EXPERTS, channel_multiplier=0,
                   allow_small_or_imprecise_dtypes=True).then_inc(consts_ready, 1)
            pool.wait_ge(z_evac, 3)
            g.affine_select(out=wT, in_=wT, compare_op=ALU.is_ge, fill=0.0, base=0,
                            pattern=[[0, GROUPS], [1, P]], channel_multiplier=-1).then_inc(masked_w, 1)

            for done in (sel_ready, gsel_ready, bsel_ready):
                pool.sem_inc(done, 1)
            pool.wait_ge(table_ready, 1)
            pool.wait_ge(gates_ready, 1)
            blk = pool.alloc_register("pool_block")
            pool.reg_mov(blk, 1)
            def turns(first, end):
                with pool.Fori(first, end) as i:
                    e = pool.value_load(order[0:1, bass.ds(i, 1)], min_val=0,
                                        max_val=EXPERTS - 1)
                    n = pool.value_load(nblk[0:1, bass.ds(i, 1)], min_val=1, max_val=MAX_BLOCKS)
                    with pool.Fori(0, n) as c:
                        prev = pool.snap(blk)
                        this = pool.snap(prev + 1)
                        pool.wait_ge(gather_full, prev)
                        pool.wait_ge(gsel_ready, prev)
                        pool.sem_inc(pool_waits, 1)
                        for m in range(TT):
                            last = g.tensor_tensor(
                                sel[:, m, :], slot_iota[:, bass.ds(c * BLK, BLK)],
                                posx[:, m, bass.ds(e, 1)].to_broadcast([P, BLK]), ALU.subtract)
                        last.then_inc(distance_ready, 1)
                        pool.wait_ge(distance_ready, prev)
                        pool.sem_inc(pool_waits, 1)
                        g.tensor_scalar(sel[:], sel[:], 0.0, None, ALU.is_equal).then_inc(sel_ready, 1)
                        pool.wait_ge(gm_full, prev)
                        pool.wait_ge(sel_ready, this)
                        pool.sem_inc(pool_waits, 1)
                        for m in range(TT):
                            last = g.tensor_tensor(
                                gsel[:, m], sel[:, m:m + 1, :].to_broadcast([P, NQ, BLK]),
                                gates[:, m, bass.ds(e, 1)].unsqueeze(2).to_broadcast([P, NQ, BLK]),
                                ALU.mult)
                        last.then_inc(gsel_ready, 1)
                        pool.wait_ge(l_full, prev)
                        pool.sem_inc(pool_waits, 1)
                        g.tensor_copy(bsel[:], ident[:, bass.ds(4 * e, 4)].unsqueeze(2)
                                      .to_broadcast([P, 4, BLK])).then_inc(bsel_ready, 1)
                        pool.reg_add(blk, blk, 1)
            turns(0, 2)
            pool.wait_ge(order_ready, 1)
            turns(2, EXPERTS)
            total = pool.snap(blk)
            pool.wait_ge(gather_full, total)
            pool.wait_ge(gsel_ready, total)
            pool.sem_inc(pool_waits, 1)
            g.memset(sel[:], 0.0).then_inc(sel_ready, 1)
            pool.wait_ge(normed, 1)
            pool.wait_ge(reloaded, 16)
            pool.sem_inc(pool_waits, 1)
            g.tensor_tensor(y_out[:, 0, :], y_out[:, 0, :], x1_back[:, 0, :],
                            ALU.add).then_inc(first_out_ready, 1)

        @block.scalar
        def _(act):
            s = nc.scalar

            def spread_vector(dst, src, done):
                act.dma_start(dst, src.rearrange("(q n) -> q n", n=QW).unsqueeze(1).to_broadcast(
                    [NQ, QUARTER, QW])).then_inc(done, 16)

            b_in = t["b_in"]
            vec_loads = [
                (V_C, 8, t["c"]), (V_GPREMIX, 8, t["g_pre_mix"]),
                (V_BQ, 4, b_in[:, 0:512]), (V_BK, 1, b_in[:, 512:640]),
                (V_BU, 4, b_in[:, 768:1280]), (V_BG, 16, b_in[:, 1792:3840])]
            for r, n, v in vec_loads:
                act.dma_start(vec_rows[r:r + n, :], v.rearrange("a (r c) -> (a r) c", c=P)
                              ).then_inc(vecs_in, 16)
            for m in range(TT):
                act.dma_start(x_sb[:, m, :], x_dram[:, m, :]).then_inc(x_in, 16)
            act.sem_inc(early_issued, 1)
            act.wait_ge(early_may_go, 1)
            b_mod = t["b_mod"][0]
            for i in range(2):
                spread_vector(mod_early[:, i * QW:(i + 1) * QW], b_mod[i * D:(i + 1) * D], bmod_in)
            act.dma_start(sg_rows, t["sg_w"].rearrange("l g t s -> t (l g) s")).then_inc(sgw_in, 16)
            act.sem_inc(early_issued, 1)

            act.wait_ge(warm_ready, 1)
            act.wait_ge(z_full, 1)
            s.copy(vecT[:, 0:V_ROWS], banks[:, 0, 0:V_ROWS]).then_inc(z_evac, 1)
            act.wait_ge(z_evac, 1)
            s.activation(csig, vecT[:, V_C:V_C + KT], ACT.Sigmoid).then_inc(csig_ready, 1)
            for m in range(TT):
                act.wait_ge(x_in, 16 * TT)
                s.activation(xn[:, m, :], x_sb[:, m, :], ACT.Square,
                             accum_out=sumsq[:, m:m + 1]).then_inc(sq_ready, 1)

            def root(n, dst, scale=1.0):
                act.wait_ge(root_in, n + 1)
                s.activation(dst, dst, ACT.Sqrt, scale=float(scale)).then_inc(root_out, 1)

            root(0, rstd)

            act.wait_ge(rest_may_go, 1)
            for dst, src in ((bias_v, b_in[:, 640:768]), (bias_vsg, b_in[:, 1280:1792]),
                             (ln_g, t["sg_ln_g"]), (ln_b, t["sg_ln_b"]), (bias_out, t["b_out"]),
                             (bias_router, t["b_router"]), (turn_rank, t["rank_of_turn"]),
                             (sink8, t["attn_sinks"])):
                act.dma_start(dst, src.to_broadcast([P, src.shape[1]])).then_inc(cols_in, 16)
            for half in range(2):
                act.dma_start(sg_bias[half * HD:(half + 1) * HD],
                              t["sg_b"].rearrange("l (j h) t -> (l h) j t", h=2)[half:half + 1]
                              .to_broadcast([HD, 4, P])).then_inc(cols_in, 16)
            act.dma_start(wr, t["w_router"][0].rearrange("(k p) e -> p k e", p=P)
                          ).then_inc(cols_in, 16)
            act.dma_start(b2_sb, t["b_mlp2"][0]).then_inc(cols_in, 16)
            act.dma_start(b1q[:], t["b_mlp1"].rearrange("l e (n c) -> (l e n) c", c=HALF)
                          ).then_inc(cols_in, 16)
            for i in range(4):
                spread_vector(mod_late[:, i // 2, (i % 2) * QW:(i % 2 + 1) * QW],
                              b_mod[D * (i + 2):D * (i + 3)], late_in)
            spread_vector(post_rows[:, 0, 0:QW], t["g_post_mix"][0], late_in)
            spread_vector(post_rows[:, 1, 0:QW], t["g_pre_ffn"][0], late_in)
            spread_vector(post_rows[:, 1, QW:2 * QW], t["g_post_ffn"][0], late_in)

            act.wait_ge(modT_full, 1)
            for i in range(2):
                last = s.copy(modT[:, KT * i:KT * (i + 1)].rearrange("p (q j) -> p j q", j=2),
                              mod_ps[:, QW * i:QW * (i + 1)].rearrange(
                                  "p (j q n) -> p j q n", j=2, q=NQ)[:, :, :, 0])
            last.then_inc(mod_ready, 1)

            act.wait_ge(xnT_full, 1)
            act.wait_ge(mod_ready, 2)
            for k in (2, 3, 6, 7):
                s.activation(hT[:, k, :], bigf[:, k * SEQ:(k + 1) * SEQ], ACT.Identity,
                             bias=modT[:, k:k + 1], scale=A1[:, k:k + 1]).then_inc(hT_act, 1)

            for half in range(2):
                act.wait_ge(z_full, 2 + half)
                s.copy(wT[:, 4 * half:4 * half + 4, :],
                       banks[:, 1 + half, :].rearrange("p (g t) -> p g t", g=4)
                       ).then_inc(z_evac, 1)

            def z_tile(r, dst, width, func, bias):
                act.wait_ge(z_full, r + 1)
                src = banks[:, r % 3, 0:width]
                if bias is None:
                    s.copy(dst, src).then_inc(z_evac, 1)
                else:
                    s.activation(dst, src, func, bias=bias).then_inc(z_evac, 1)

            def gate_tile(j):
                z_tile(15 + j, gate_sig[:, j, :], SEQ, ACT.Sigmoid, vecT[:, V_BG + j:V_BG + j + 1])

            def exps(b, L):
                act.wait_ge(negm_ready, 2 * b + 1)
                for h in range(HEADS):
                    last = s.activation(L[:, h, :], L[:, h, :], ACT.Exp, scale=0.125,
                                        bias=negm[:, b, h:h + 1], accum_out=den[:, b, h:h + 1])
                last.then_inc(probs_exp, 1)
                act.wait_ge(negm_ready, 2 * b + 2)
                s.activation(sinkp[:, b, :], sinkp[:, b, :], ACT.Exp).then_inc(sink_exp, 1)

            for j in range(4):
                z_tile(3 + j, qT[:, j, :], SEQ, ACT.Identity, vecT[:, V_BQ + j:V_BQ + j + 1])
            z_tile(7, kT, SEQ, ACT.Identity, vecT[:, V_BK:V_BK + 1])
            act.wait_ge(z_evac, 8)
            s.copy(kT_swapped[0:HD, :], kT[HD:P, :])
            s.copy(kT_swapped[HD:P, :], kT[0:HD, :]).then_inc(k_swapped, 1)
            z_tile(8, v_tok.rearrange("p t c -> p (t c)"), SEQ, None, None)
            for j in range(4):
                z_tile(9 + j, uT[:, j, :], SEQ, ACT.Gelu_apprx_tanh, vecT[:, V_BU + j:V_BU + j + 1])
            for m in range(TT):
                z_tile(13 + m, v_sg[:, m, :], SGW, None, None)
            act.wait_ge(vsg_biased, TT)
            for m in range(TT):
                s.activation(v_sg[:, m, :], v_sg[:, m, :], ACT.Gelu_apprx_tanh).then_inc(vsg_gelu, 1)
            for j in range(2):
                gate_tile(j)
            exps(0, L1)
            exps(1, L0)
            root(1, ln_rstd)
            for j in range(2, 16):
                gate_tile(j)

            for r in range(3):
                act.wait_ge(pT_full, r + 1)
                b = 2 * (r % 2)
                s.copy(pT[:, 8 * r:8 * r + 8, :].rearrange("p i q -> p (i q)"),
                       bigf[:, b * 512:(b + 2) * 512]).then_inc(pT_evac, 1)
            act.wait_ge(att_full, 1)
            s.copy(yattT.rearrange("p j s -> p (j s)"), bigf[:, 1024:2048]).then_inc(att_evac, 1)

            for i in range(2):
                act.wait_ge(rowb_full, i + 1)
                act.wait_ge(ysg_ready, 1)
                for j, r in enumerate(((0, 2), (1, 3))[i]):
                    s.copy(rows[:, r, :].rearrange("p (q n) -> p q n", q=NQ),
                           big[:, :, j * QW:(j + 1) * QW]).then_inc(rowb_evac, 1)

            def squares(src, m, sums_of, ready, scratch, done):
                for h in range(2):
                    c = slice(h * HALF, (h + 1) * HALF)
                    act.wait_ge(ready, 2 * m + h + 1)
                    s.activation(scratch[:, m, c], src[:, m, c], ACT.Square,
                                 accum_out=sums_of[:, 2 * m + h:2 * m + h + 1]).then_inc(done, 1)

            def h2T_quarter(i):
                act.wait_ge(h2T_full, i + 1)
                m, k = i // 2, slice(4 * (i % 2), 4 * (i % 2) + 4)
                s.copy(hT[:, k, m * P:(m + 1) * P], h2T_ps[:, m, k, :]).then_inc(h2T_evac, 1)

            for m in range(TT):
                squares(xn, m, sumsq_y, y_biased, h2, ysq_ready)
                root(2 + 2 * m, rstd_y[:, m:m + 1], D)
                if m == TT - 1:
                    h2T_quarter(0)
                    h2T_quarter(1)
                squares(x_sb, m, sumsq_x1, x1_ready, xn, x1sq_ready)
                root(3 + 2 * m, rstd_x1[:, m:m + 1], D)
            h2T_quarter(2)
            s.activation(warm, warm, ACT.Exp).then_inc(act_step, 1)
            act.wait_ge(negtop_ready, 1)
            for m in range(TT):
                last = s.activation(gates[:, m, :], padded[:, m, 0:EXPERTS], ACT.Exp,
                                    bias=negtop[:, m:m + 1])
            last.then_inc(gexp_ready, 1)
            act.wait_ge(gT_full, 1)
            s.copy(gT.rearrange("p t q -> p (t q)"),
                   banks[0:EXPERTS, 3, 0:SEQ]).then_inc(gT_ready, 1)

            for done in (xg_evac, xgT_ready, sig_ready, actT_ready):
                act.sem_inc(done, 1)
            act.wait_ge(table_ready, 1)
            blk = act.alloc_register("act_block")
            act.reg_mov(blk, 1)

            def gathered(count, read):
                act.wait_ge(gather_full, count)
                act.wait_ge(xturn_full, read)
                s.copy(xg_rows, bank_x).then_inc(xg_evac, 1)
                act.wait_ge(xturn_full, count)
                act.wait_ge(l_full, read)
                s.copy(xgT, bank_y).then_inc(xgT_ready, 1)

            gathered(2, 1)
            def turns(first, end):
                with act.Fori(first, end) as i:
                    n = act.value_load(nblk[0:1, bass.ds(i, 1)], min_val=1, max_val=MAX_BLOCKS)
                    with act.Fori(0, n) as _c:
                        prev = act.snap(blk)
                        this = act.snap(prev + 1)
                        act.wait_ge(g_ready, this)
                        act.wait_ge(act_ready, prev)
                        s.activation(sig, gbuf, ACT.Sigmoid, scale=ALPHA).then_inc(sig_ready, 1)
                        gathered(act.snap(prev + 2), this)
                        act.wait_ge(gm_full, this)
                        act.wait_ge(combined, this)
                        s.copy(gm[:].rearrange("p t q -> p (t q)"), turned_g).then_inc(gm_ready, 1)
                        act.wait_ge(aturn_full, this)
                        act.wait_ge(res_full, prev)
                        s.copy(actT, bank_l).then_inc(actT_ready, 1)
                        act.wait_ge(res_full, this)
                        act.wait_ge(combined, this)
                        s.copy(y_sb, bank_y).then_inc(res_ready, 1)
                        act.reg_add(blk, blk, 1)

            turns(0, 2)
            act.wait_ge(order_ready, 1)
            turns(2, EXPERTS)
            total = act.snap(blk)
            act.wait_ge(act_step, 1)
            s.activation(warm, warm, ACT.Sqrt)
            act.wait_ge(combined, total + 1)
            act.wait_ge(reloaded, 16)
            for m in range(TT):
                s.activation(fsq_scratch[:, m, :].rearrange("p (q n) -> p q n", q=NQ),
                             sums[:, :, m, :], ACT.Square,
                             accum_out=sumsq_f[:, m:m + 1]).then_inc(fsq_ready, 1)
            root(6, rstd_f)

        @block.vector
        def _(dve):
            v = nc.vector
            steps = [0]

            def link(ins):
                steps[0] += 1
                ins.then_inc(dve_step, 1)
                dve.wait_ge(dve_step, steps[0])

            roots = [0]

            def rstd_of(dst, sq, n):
                link(v.tensor_scalar(dst, sq, 1.0 / n, EPS, ALU.mult, ALU.add))
                v.reciprocal(dst, dst).then_inc(root_in, 1)
                roots[0] += 1
                dve.wait_ge(root_out, roots[0])

            v.memset(padded, FAR)
            v.memset(warm, 1.0).then_inc(warm_ready, 1)
            dve.wait_ge(csig_ready, 1)
            v.tensor_tensor(cact, vecT[:, V_C:V_C + KT], csig, ALU.mult).then_inc(cact_ready, 1)
            dve.wait_ge(sq_ready, TT)
            rstd_of(rstd, sumsq, D)
            for m in range(TT):
                v.tensor_scalar(xn[:, m, :], x_sb[:, m, :], rstd[:, m:m + 1], None,
                                ALU.mult).then_inc(xn_ready, 1)
            dve.wait_ge(mod_full, 2)
            dve.wait_ge(bmod_in, 16 * 2)
            v.tensor_tensor(mod_early, mod_early, mod_ps, ALU.add).then_inc(mod_evac, 1)
            dve.wait_ge(mod_ready, 1)
            v.scalar_tensor_tensor(out=A1, in0=modT[:, 8:16], scalar=1.0,
                                   in1=vecT[:, V_GPREMIX:V_GPREMIX + KT],
                                   op0=ALU.add, op1=ALU.mult).then_inc(mod_ready, 1)
            dve.wait_ge(mod_ready, 2)
            dve.wait_ge(xnT_full, 1)
            for k in (0, 1, 4, 5):
                v.tensor_scalar(hT[:, k, :], bigf[:, k * SEQ:(k + 1) * SEQ], A1[:, k:k + 1],
                                modT[:, k:k + 1], ALU.mult, ALU.add).then_inc(hT_dve, 1)
            dve.wait_ge(cols_in, 16 * 13)
            link(v.tensor_scalar(sink8, sink8, 8.0, None, ALU.mult))
            dve.wait_ge(z_evac, 9)
            v.tensor_tensor(v_tok, v_tok, bias_v.unsqueeze(1).to_broadcast([P, TT, P]),
                            ALU.add).then_inc(v_ready, 1)

            def logits(b, L, src, dist_b):
                dve.wait_ge(scores_full, b + 1)
                for h in range(HEADS):
                    slope = 2.0 ** (-8.0 * (h + 1) / HEADS)
                    last = v.scalar_tensor_tensor(out=L[:, h, :], in0=dist_b, scalar=-8.0 * slope,
                                                  in1=src[:, (h % 2) * 4 + h // 2, :],
                                                  op0=ALU.mult, op1=ALU.add)
                last.then_inc(logits_ready, 1)
                dve.wait_ge(logits_ready, b + 1)
                link(v.tensor_reduce(mx[:, b, :], L, AX.X, ALU.max))
                link(v.tensor_tensor(mx[:, b, :], mx[:, b, :], sink8, ALU.max))
                v.tensor_scalar(negm[:, b, :], mx[:, b, :], -0.125, None,
                                ALU.mult).then_inc(negm_ready, 1)
                dve.wait_ge(negm_ready, 2 * b + 1)
                v.scalar_tensor_tensor(out=sinkp[:, b, :], in0=sink8, scalar=0.125,
                                       in1=negm[:, b, :], op0=ALU.mult,
                                       op1=ALU.add).then_inc(negm_ready, 1)

            def probs(b, L, width):
                dve.wait_ge(probs_exp, b + 1)
                dve.wait_ge(sink_exp, b + 1)
                link(v.tensor_tensor(den[:, b, :], den[:, b, :], sinkp[:, b, :], ALU.add))
                link(v.reciprocal(den[:, b, :], den[:, b, :]))
                v.tensor_tensor(L, L, den[:, b, :].unsqueeze(2).to_broadcast([P, HEADS, width]),
                                ALU.mult).then_inc(probs_ready, 1)

            dve.wait_ge(consts_ready, 4)
            v.tensor_scalar(ends, slot_iota[:, 1:MAX_BLOCKS], float(BLK), 0.5, ALU.mult, ALU.add)
            logits(0, L1, bigf.rearrange("p (h k) -> p h k", h=HEADS), dist)
            dve.wait_ge(z_evac, 15)
            for m in range(TT):
                v.tensor_tensor(v_sg[:, m, :], v_sg[:, m, :], bias_vsg,
                                ALU.add).then_inc(vsg_biased, 1)
            logits(1, L0, bigf[:, 0:1024].rearrange("p (h k) -> p h k", h=HEADS), dist[:, P:2 * P])
            for m in range(TT):
                dve.wait_ge(vsg_gelu, m + 1)
                link(v.bn_stats(stats[:, m, :], v_sg[:, m, :]))
                link(v.bn_aggr(mv[:, m, :], stats[:, m, :]))
            rstd_of(ln_rstd, mv[:, :, 1], 1)
            for m in range(TT):
                link(v.tensor_scalar(v_sg[:, m, :], v_sg[:, m, :], mv[:, m, 0:1],
                                     ln_rstd[:, m:m + 1], ALU.subtract, ALU.mult))
                link(v.tensor_tensor(v_sg[:, m, :], v_sg[:, m, :], ln_g, ALU.mult))
                v.tensor_tensor(v_sg[:, m, :], v_sg[:, m, :], ln_b, ALU.add).then_inc(vsg_ready, 1)
            probs(0, L1, 2 * P)
            probs(1, L0, P)

            dve.wait_ge(late_in, 16 * 7)
            dve.wait_ge(mod_full, 4)
            link(v.tensor_tensor(mod_late[:, 0, :], mod_late[:, 0, :], mod_ps, ALU.add))
            dve.sem_inc(mod_evac, 1)
            v.tensor_tensor(mod_late[:, 0, 0:QW], mod_late[:, 0, 0:QW], post_rows[:, 0, 0:QW],
                            ALU.mult).then_inc(mod_rows_ready, 1)

            dve.wait_ge(mix_full, 1)
            link(v.tensor_tensor(
                ysgT.rearrange("p j (b q) -> p j b q", b=2),
                bigf[:, 0:1024].rearrange("p (j b q) -> p j b q", j=4, b=2),
                sg_bias.unsqueeze(2).to_broadcast([P, 4, 2, P]), ALU.add))
            v.tensor_tensor(ysgT, ysgT, uT, ALU.mult).then_inc(ysg_ready, 1)

            dve.wait_ge(mod_full, 6)
            link(v.tensor_tensor(mod_late[:, 1, :], mod_late[:, 1, :], mod_ps, ALU.add))
            v.scalar_tensor_tensor(out=mod_late[:, 1, 0:QW], in0=mod_late[:, 1, 0:QW], scalar=1.0,
                                   in1=post_rows[:, 1, 0:QW], op0=ALU.add, op1=ALU.mult)
            v.tensor_tensor(mod_late[:, 1, QW:2 * QW], mod_late[:, 1, QW:2 * QW],
                            post_rows[:, 1, QW:2 * QW], ALU.mult).then_inc(mod_rows_ready, 1)

            for n in range(KT):
                dve.wait_ge(br_full, n + 1)
                if n:
                    dve.wait_ge(merged_ready, n)
                src = banks[:, n % 3, :]
                v.tensor_tensor(mT[:, n, :], src[:, 0:SEQ], gate_sig[:, n, :],
                                ALU.mult).then_inc(dve_step, 1)
                v.tensor_tensor(branch, src[:, SEQ:2 * SEQ], gate_sig[:, 8 + n, :],
                                ALU.mult).then_inc(dve_step, 1)
                steps[0] += 2
                dve.wait_ge(dve_step, steps[0])
                v.tensor_tensor(mT[:, n, :], mT[:, n, :], branch, ALU.add).then_inc(merged_ready, 1)

            dve.wait_ge(rowb_evac, 4)
            def mark(ins):
                steps[0] += 1
                ins.then_inc(dve_step, 1)
                return steps[0]

            def rstd_of_halves(dst, sq):
                link(v.scalar_tensor_tensor(out=dst, in0=sq[:, 0:1], scalar=D * EPS, in1=sq[:, 1:2],
                                            op0=ALU.add, op1=ALU.add))
                v.reciprocal(dst, dst).then_inc(root_in, 1)
                roots[0] += 1
                dve.wait_ge(root_out, roots[0])

            halves = [slice(h * HALF, (h + 1) * HALF) for h in range(2)]
            for m in range(TT):
                one, two = slice(m, m + 1), slice(2 * m, 2 * m + 2)
                for h, c in enumerate(halves):
                    dve.wait_ge(y_full, 2 * m + h + 1)
                    v.tensor_tensor(xn[:, m, c], y_ps[:, m, c], bias_out[:, c],
                                    ALU.add).then_inc(y_biased, 1)
                dve.wait_ge(ysq_ready, 2 * m + 2)
                rstd_of_halves(rstd_y[:, one], sumsq_y[:, two])
                at = [mark(v.scalar_tensor_tensor(out=xn[:, m, c], in0=xn[:, m, c],
                                                  scalar=rstd_y[:, one], in1=rows[:, 0, c],
                                                  op0=ALU.mult, op1=ALU.mult)) for c in halves]
                for h, c in enumerate(halves):
                    dve.wait_ge(dve_step, at[h])
                    v.tensor_tensor(x_sb[:, m, c], x_sb[:, m, c], xn[:, m, c],
                                    ALU.add).then_inc(x1_ready, 1)
                dve.wait_ge(x1sq_ready, 2 * m + 2)
                rstd_of_halves(rstd_x1[:, one], sumsq_x1[:, two])
                at = [mark(v.scalar_tensor_tensor(out=h2[:, m, c], in0=x_sb[:, m, c],
                                                  scalar=rstd_x1[:, one], in1=rows[:, 1, c],
                                                  op0=ALU.mult, op1=ALU.mult)) for c in halves]
                for h, c in enumerate(halves):
                    dve.wait_ge(dve_step, at[h])
                    v.tensor_tensor(h2[:, m, c], h2[:, m, c], rows[:, 2, c],
                                    ALU.add).then_inc(h2_ready, 1)
            dve.wait_ge(h2T_full, 4)
            v.tensor_copy(hT[:, 4:8, P:2 * P], h2T_ps[:, 1, 4:8, :]).then_inc(h2T_dve, 1)

            dve.wait_ge(logits_full, 1)
            lg = padded[:, :, 0:EXPERTS]
            v.tensor_tensor(lg, banks[:, 1, 0:TT * EXPERTS].rearrange("p (t e) -> p t e", t=TT),
                            bias_router.unsqueeze(1).to_broadcast([P, TT, EXPERTS]),
                            ALU.add).then_inc(lg_ready, 1)
            dve.wait_ge(lg_ready, 1)
            dve.sem_inc(front_done, 1)
            wide = [P, TT, EXPERTS]
            for m in range(TT):
                last = v.max(largest[:, m, :], padded[:, m, :])
            link(last)
            v.tensor_scalar(negtop, largest[:, :, TOP_K], -1.0, None,
                            ALU.mult).then_inc(negtop_ready, 1)
            dve.wait_ge(gexp_ready, 1)
            for m in range(TT):
                last = v.match_replace(padded[:, m, :], largest[:, m, :], padded[:, m, :], MASKED)
            link(last)
            v.tensor_scalar(chosen, lg, MASKED, None, ALU.is_equal).then_inc(chosen_ready, 1)
            dve.wait_ge(chosen_ready, 1)
            v.memset(y_sb, 0.0).then_inc(res_ready, 1)
            v.memset(gm[:], 0.0).then_inc(gm_ready, 1)
            link(v.tensor_tensor(gates[:], gates[:], chosen, ALU.mult))
            link(v.tensor_reduce(gsum, gates[:], AX.X, ALU.add))
            link(v.reciprocal(gsum, gsum))
            v.tensor_tensor(gates[:], gates[:], gsum.unsqueeze(2).to_broadcast(wide),
                            ALU.mult).then_inc(gates_ready, 1)
            dve.wait_ge(pos_full, 1)
            pos_ps = banks[:, 2, 0:3 * EXPERTS].rearrange("p (t e) -> p t e", t=3)
            link(v.tensor_scalar(posx[:], pos_ps[:, 0:TT, :], UNROUTED, None, ALU.add))
            link(v.scalar_tensor_tensor(out=posx[:], in0=chosen, scalar=-UNROUTED, in1=posx[:],
                                        op0=ALU.mult, op1=ALU.add))
            post_flat = post_rows[:].rearrange("p i n -> p (i n)")
            full_blocks = post_flat[:, 0:EXPERTS * (MAX_BLOCKS - 1)].rearrange(
                "p (e j) -> p e j", e=EXPERTS)
            over = [P, EXPERTS, MAX_BLOCKS - 1]
            link(v.tensor_tensor(full_blocks, pos_ps[:, 2, :].unsqueeze(2).to_broadcast(over),
                                 ends.unsqueeze(1).to_broadcast(over), ALU.is_gt))
            link(v.tensor_reduce(blocks_f, full_blocks, AX.X, ALU.add))
            link(v.tensor_scalar(blocks_f, blocks_f, 1.0, None, ALU.add))
            link(v.scalar_tensor_tensor(out=key, in0=pos_ps[:, 2, 2:EXPERTS], scalar=float(EXPERTS),
                                        in1=revidx[:, 2:EXPERTS], op0=ALU.mult, op1=ALU.add))
            v.tensor_copy(nblk[:, 0:2], blocks_f[:, 0:2])
            v.tensor_copy(order[:, 0:2], slot_iota[:, 0:2]).then_inc(table_ready, 1)

            R = RANKS
            square = [P, R, R]
            grid = post_flat[:, 0:R * R].rearrange("p (a b) -> p a b", a=R)
            link(v.tensor_tensor(grid, key.unsqueeze(1).to_broadcast(square),
                                 key.unsqueeze(2).to_broadcast(square), ALU.is_gt))
            link(v.tensor_reduce(rank, grid, AX.X, ALU.add))
            for table, values in ((order, slot_iota[:, 2:EXPERTS]), (nblk, blocks_f[:, 2:EXPERTS])):
                link(v.tensor_tensor(grid, turn_rank.unsqueeze(2).to_broadcast(square),
                                     rank.unsqueeze(1).to_broadcast(square), ALU.is_equal))
                link(v.tensor_tensor(grid, grid, values.unsqueeze(1).to_broadcast(square),
                                     ALU.mult))
                link(v.tensor_reduce(key, grid, AX.X, ALU.add))
                link(v.tensor_copy(table[:, 2:EXPERTS], key))
            dve.sem_inc(order_ready, 1)

            for done in (g_ready, l_ready, gl_ready, act_ready):
                dve.sem_inc(done, 1)
            blk = dve.alloc_register("dve_block")
            dve.reg_mov(blk, 1)
            def turns(first, end):
                with dve.Fori(first, end) as i:
                    n = dve.value_load(nblk[0:1, bass.ds(i, 1)], min_val=1, max_val=MAX_BLOCKS)
                    with dve.Fori(0, n) as _c:
                        prev = dve.snap(blk)
                        this = dve.snap(prev + 1)
                        dve.wait_ge(g_full, this)
                        v.tensor_scalar(gbuf, bank_g, LIMIT, None, ALU.min).then_inc(g_ready, 1)
                        dve.wait_ge(l_full, this)
                        dve.wait_ge(act_ready, prev)
                        v.tensor_scalar(lbuf, bank_l, LIMIT, -LIMIT, ALU.min,
                                        ALU.max).then_inc(l_ready, 1)
                        dve.wait_ge(l_ready, this)
                        dve.wait_ge(g_ready, this)
                        v.scalar_tensor_tensor(out=lbuf, in0=lbuf, scalar=1.0, in1=gbuf, op0=ALU.add,
                                               op1=ALU.mult).then_inc(gl_ready, 1)
                        dve.wait_ge(gl_ready, this)
                        dve.wait_ge(sig_ready, this)
                        v.tensor_tensor(lbuf, lbuf, sig, ALU.mult).then_inc(act_ready, 1)
                        dve.reg_add(blk, blk, 1)

            turns(0, 2)
            dve.wait_ge(order_ready, 1)
            turns(2, EXPERTS)
            dve.wait_ge(fsq_ready, TT)
            rstd_of(rstd_f, sumsq_f, D)
            dve.wait_ge(reloaded, 16)
            for m in range(TT):
                v.scalar_tensor_tensor(
                    out=y_out[:, m, :].rearrange("p (q n) -> p q n", q=NQ), in0=sums[:, :, m, :],
                    scalar=rstd_f[:, m:m + 1], in1=row_back.rearrange("p (q n) -> p q n", q=NQ),
                    op0=ALU.mult, op1=ALU.mult).then_inc(normed, 1)
            dve.wait_ge(normed, TT)
            for c in halves:
                v.tensor_tensor(y_out[:, TT - 1, c], y_out[:, TT - 1, c], x1_back[:, TT - 1, c],
                                ALU.add).then_inc(out_ready, 1)

        @block.tensor
        def _(pe):
            mm, tr = nc.tensor.matmul, nc.tensor.transpose

            def piece_in(n):
                pe.wait_ge(slot_full[n % FRONT_SLOTS], 16 * (n // FRONT_SLOTS + 1))
                return W[:, n % FRONT_SLOTS]

            pe.wait_ge(consts_ready, 1)
            pe.wait_ge(vecs_in, 16 * 6)
            tr(banks[:, 0, 0:V_ROWS], vec_rows[0:V_ROWS, :],
               ident[0:V_ROWS, 0:V_ROWS]).then_inc(z_full, 1)
            def modulation(i, n):
                w = piece_in(n)
                at = (i % 2) * QW
                for k in range(KT):
                    if k == 4 and n in MOD_EARLY:
                        pe.wait_ge(mod_rest_full[n], 16)
                    for q in range(NQ):
                        last = mm(mod_ps[q * QUARTER:(q + 1) * QUARTER, at:at + QW],
                                  cact[:, k:k + 1].to_broadcast([P, QUARTER]),
                                  w[:, k, q * QW:(q + 1) * QW], start=(k == 0),
                                  stop=(k == KT - 1))
                last.then_inc(mod_full, 1)

            pe.wait_ge(cact_ready, 1)
            modulation(0, MOD_EARLY[0])
            pe.wait_ge(xn_ready, TT)
            for k in range(KT):
                for m in range(TT):
                    last = tr(bigf[:, k * SEQ + m * P:k * SEQ + (m + 1) * P],
                              xn[:, m, k * P:(k + 1) * P], ident[:])
            last.then_inc(xnT_full, 1)
            modulation(1, MOD_EARLY[1])
            pe.wait_ge(mod_evac, 1)
            for j in range(4):
                last = tr(mod_ps[:, j * P:(j + 1) * P], mod_early[:, j * P:(j + 1) * P], ident[:])
            last.then_inc(modT_full, 1)
            pe.wait_ge(sgw_in, 16)
            for half in range(2):
                for g in range(4):
                    last = tr(banks[:, 1 + half, g * P:(g + 1) * P],
                              sg_rows[:, 4 * half + g, :], ident[:])
                last.then_inc(z_full, 1)

            def z_bank(r):
                pe.wait_ge(z_evac, r - 2)
                return banks[:, r % 3, :]

            def z_transposed(r, w, cols):
                b = z_bank(r)
                for k in range(KT):
                    if r == 3:
                        pe.wait_ge((hT_dve, hT_act)[k // 2 % 2], k // 4 * 2 + k % 2 + 1)
                    last = mm(b[:, 0:SEQ], w[:, k, cols], hT[:, k, :], start=(k == 0),
                              stop=(k == KT - 1))
                last.then_inc(z_full, 1)

            w = piece_in(IN_PIECES[0])
            for j in range(4):
                z_transposed(3 + j, w, slice(j * P, (j + 1) * P))
            pe.wait_ge(in_rest_full, 16)
            z_transposed(7, w, slice(512, 640))
            b = z_bank(8)
            for m in range(TT):
                for k in range(KT):
                    last = mm(b[:, m * P:(m + 1) * P], hT[:, k, m * P:(m + 1) * P],
                              w[:, k, 640:768], start=(k == 0), stop=(k == KT - 1))
            last.then_inc(z_full, 1)
            for j in range(2):
                z_transposed(9 + j, w, slice(768 + j * P, 768 + (j + 1) * P))

            def scores(b, width):
                pe.wait_ge(z_evac, 8)
                pe.wait_ge(k_swapped, 1)
                q = slice(P, 2 * P) if b == 0 else slice(0, P)
                for h in range(HEADS):
                    part = slice((h % 2) * HD, (h % 2 + 1) * HD)
                    keys = kT if h % 2 == h // 4 else kT_swapped
                    at = ((h % 2) * 4 + h // 2) * width
                    last = mm(bigf[:, at:at + width], qT[part, h // 2, q],
                              keys[part, 0:width], start=True, stop=True)
                last.then_inc(scores_full, 1)

            scores(0, 2 * P)
            w = piece_in(IN_PIECES[1])
            for j in range(2):
                z_transposed(11 + j, w, slice(j * P, (j + 1) * P))
            for m in range(TT):
                b = z_bank(13 + m)
                for k in range(KT):
                    last = mm(b, hT[:, k, m * P:(m + 1) * P], w[:, k, 256:768], start=(k == 0),
                              stop=(k == KT - 1))
                last.then_inc(z_full, 1)
            for j in range(2):
                z_transposed(15 + j, w, slice(768 + j * P, 768 + (j + 1) * P))
            pe.wait_ge(logits_ready, 1)
            scores(1, P)
            pe.wait_ge(mod_ready, 1)
            modulation(2, MOD_LATE[0])
            w = piece_in(IN_PIECES[2])
            for j in range(8):
                z_transposed(17 + j, w, slice(j * P, (j + 1) * P))
            modulation(3, MOD_LATE[1])
            w = piece_in(IN_PIECES[3])
            for j in range(6):
                z_transposed(25 + j, w, slice(j * P, (j + 1) * P))
            pe.wait_ge(mod_evac, 2)
            modulation(4, MOD_LATE[2])

            pe.wait_ge(probs_ready, 2)
            tiles = [L0[:, h, :] for h in range(HEADS)] + [
                L1[:, h, kb * P:(kb + 1) * P] for h in range(HEADS) for kb in range(2)]
            for r in range(3):
                if r == 0:
                    pe.wait_ge(logits_ready, 2)
                if r == 2:
                    pe.wait_ge(pT_evac, 1)
                b = 1024 * (r % 2)
                for i in range(8):
                    last = tr(bigf[:, b + i * P:b + (i + 1) * P], tiles[8 * r + i], ident[:])
                last.then_inc(pT_full, 1)
            pe.wait_ge(v_ready, 1)
            pe.wait_ge(pT_evac, 3)
            for h in range(HEADS):
                vh = slice((h // 4) * HD, (h // 4 + 1) * HD)
                rows_h = slice((h % 2) * HD, (h % 2 + 1) * HD)
                at = 1024 + (h // 2) * SEQ
                mm(bigf[rows_h, at:at + P], v_tok[:, 0, vh], pT[:, h, :], start=True, stop=True)
                for kb in range(2):
                    last = mm(bigf[rows_h, at + P:at + 2 * P], v_tok[:, kb, vh],
                              pT[:, 8 + 2 * h + kb, :], start=(kb == 0), stop=(kb == 1))
            last.then_inc(att_full, 1)
            pe.wait_ge(vsg_ready, TT)
            pe.wait_ge(masked_w, 1)
            for g in range(GROUPS):
                rows_g = slice((g % 2) * HD, (g % 2 + 1) * HD)
                for m in range(TT):
                    at = (g // 2) * SEQ + m * P
                    last = mm(bigf[rows_g, at:at + P], v_sg[:, m, g * HD:(g + 1) * HD], wT[:, g, :],
                              start=True, stop=True)
            last.then_inc(mix_full, 1)
            modulation(5, MOD_LATE[3])

            def spread_over_partitions(i):
                pe.wait_ge(mod_rows_ready, i + 1)
                for q in range(NQ):
                    row = slice(q * QUARTER, q * QUARTER + 1)
                    last = mm(big[:, q, :], ones[row, :], mod_late[row, i, :], start=True, stop=True)
                last.then_inc(rowb_full, 1)

            pe.wait_ge(att_evac, 1)
            pe.wait_ge(ysg_ready, 1)
            spread_over_partitions(0)

            w = piece_in(BR_PIECE)
            pe.wait_ge(br_sg_full, 16)
            pe.wait_ge(z_evac, 31)
            for n in range(KT):
                if n >= 3:
                    pe.wait_ge(merged_ready, n - 2)
                if n == 2:
                    pe.wait_ge(rowb_evac, 2)
                    spread_over_partitions(1)
                for side, src in ((0, yattT), (1, ysgT)):
                    for k in range(4):
                        last = mm(banks[:, n % 3, side * SEQ:(side + 1) * SEQ],
                                  w[:, 4 * side + k, n * P:(n + 1) * P], src[:, k, :],
                                  start=(k == 0), stop=(k == 3))
                last.then_inc(br_full, 1)
            w = piece_in(OUT_PIECE)
            pe.wait_ge(merged_ready, KT)
            pe.wait_ge(rowb_evac, 4)
            for m in range(TT):
                for h in range(2):
                    c = slice(h * 512, (h + 1) * 512)
                    for k in range(KT):
                        last = mm(y_ps[:, m, c], mT[:, k, m * P:(m + 1) * P], w[:, k, c],
                                  start=(k == 0), stop=(k == KT - 1))
                    last.then_inc(y_full, 1)

            for m in range(TT):
                for h in range(2):
                    pe.wait_ge(h2_ready, 2 * m + h + 1)
                    for k in range(4 * h, 4 * h + 4):
                        last = tr(h2T_ps[:, m, k, :], h2[:, m, k * P:(k + 1) * P], ident[:])
                    last.then_inc(h2T_full, 1)
                for k in range(KT):
                    if k % 4 == 0:
                        i = 2 * m + k // 4
                        if i < 3:
                            pe.wait_ge(h2T_evac, i + 1)
                        else:
                            pe.wait_ge(h2T_dve, 1)
                    last = mm(banks[:, 1, m * EXPERTS:(m + 1) * EXPERTS],
                              hT[:, k, m * P:(m + 1) * P], wr[:, k, :], start=(k == 0),
                              stop=(k == KT - 1))
            last.then_inc(logits_full, 1)
            pe.wait_ge(chosen_ready, 1)
            pe.wait_ge(consts_ready, 5)
            E = EXPERTS
            mm(banks[:, 2, 0:E], U, chosen[:, 0, :], start=True, stop=True)
            mm(banks[:, 2, E:2 * E], ones, chosen[:, 0, :], start=True, stop=False)
            mm(banks[:, 2, E:2 * E], U, chosen[:, 1, :], start=False, stop=True)
            mm(banks[:, 2, 2 * E:3 * E], ones, chosen[:, 0, :], start=True, stop=False)
            mm(banks[:, 2, 2 * E:3 * E], ones, chosen[:, 1, :], start=False,
               stop=True).then_inc(pos_full, 1)
            pe.wait_ge(gates_ready, 1)
            for m in range(TT):
                last = tr(banks[0:E, 3, m * P:(m + 1) * P], gates[:, m, :], ident[:])
            last.then_inc(gT_full, 1)
            pe.wait_ge(gT_ready, 1)
            def open_sums(quarters):
                for q in quarters:
                    for m in range(TT):
                        last = mm(sums[:, q, m, :], gT[:, m, :], b2_sb[:, q * QW:(q + 1) * QW],
                                  start=(m == 0), stop=False, skip_group_check=True)
                return last

            open_sums((0, 1))

            for done in (xturn_full, gm_full, g_full, l_full, aturn_full, res_full, combined,
                         gather_full):
                pe.sem_inc(done, 1)
            pe.wait_ge(table_ready, 1)
            blk = pe.alloc_register("pe_block")
            pe.reg_mov(blk, 1)
            part = [slice(q * BLK, (q + 1) * BLK) for q in range(NQ)]
            cols = [slice(q * QW, (q + 1) * QW) for q in range(NQ)]

            def gather():
                for m in range(TT):
                    for q in range(NQ):
                        last = mm(bank_x[part[q], :], sel[:, m, :], h2[:, m, cols[q]],
                                  start=(m == 0), stop=(m == TT - 1))
                last.then_inc(gather_full, 1)

            def combine(stop):
                for m in range(TT):
                    for q in range(NQ):
                        last = mm(sums[:, q, m, :], gm[part[q], m, :], y_sb[part[q], :],
                                  start=False, stop=stop, skip_group_check=True)
                last.then_inc(combined, 1)

            def turn(bank, rows_sb, full):
                for j in range(2):
                    last = tr(bank[:, j * P:(j + 1) * P], rows_sb[:, j * P:(j + 1) * P], ident[:])
                last.then_inc(full, 1)

            def layer(bank, w, turned, bias_row, full, rest=None):
                if bias_row is not None:
                    for q in range(NQ):
                        mm(bank[part[q], :], bsel[:, bias_row + q // 2, :],
                           b1q[:, (q % 2) * QW:(q % 2 + 1) * QW], start=True, stop=False)
                for k in range(KT):
                    if k == 4 and rest is not None:
                        pe.wait_ge(*rest)
                    at = (k % 2) * P + (k // 2) * BLK
                    for q in range(NQ):
                        last = mm(bank[part[q], :], turned[:, at:at + BLK], w[:, k, cols[q]],
                                  start=(bias_row is None and k == 0), stop=(k == KT - 1))
                last.then_inc(full, 1)

            def expert_block(base, full, full_rest):
                prev = pe.snap(blk)
                this = pe.snap(prev + 1)
                following = pe.snap(prev + 2)
                pe.wait_ge(gm_ready, prev)
                pe.wait_ge(bsel_ready, this)
                pe.wait_ge(xgT_ready, this)
                pe.wait_ge(slot_full[base], full)
                layer(bank_g, W[:, base], xgT, 0, g_full)
                pe.wait_ge(sel_ready, following)
                gather()
                pe.wait_ge(actT_ready, prev)
                pe.wait_ge(slot_full[base + 1], full)
                layer(bank_l, W[:, base + 1], xgT, 2, l_full)
                pe.wait_ge(res_ready, prev)
                combine(False)
                pe.wait_ge(xg_evac, following)
                turn(bank_y, xg_rows, xturn_full)
                pe.wait_ge(g_ready, this)
                pe.wait_ge(gsel_ready, this)
                for m in range(TT):
                    last = tr(turned_g[:, m * P:(m + 1) * P],
                              gsel[:, m].rearrange("p a s -> p (a s)"), ident[:])
                last.then_inc(gm_full, 1)
                pe.wait_ge(act_ready, this)
                turn(bank_l, lbuf, aturn_full)
                pe.wait_ge(actT_ready, this)
                pe.wait_ge(xgT_ready, following)
                pe.wait_ge(slot_full[base + 2], full)
                layer(bank_y, W[:, base + 2], actT, None, res_full,
                      (w2_rest_full[base // 3], full_rest))
                pe.reg_add(blk, blk, 1)

            pe.wait_ge(sel_ready, 2)
            gather()
            open_sums((2,))
            pe.wait_ge(xg_evac, 2)
            turn(bank_y, xg_rows, xturn_full)
            open_sums((3,)).then_inc(sums_open, 1)
            pe.wait_ge(sums_open, 1)
            def turns(i):
                for half in range(2):
                    n = pe.value_load(nblk[0:1, bass.ds(2 * i + half, 1)], min_val=1,
                                      max_val=MAX_BLOCKS)
                    first = FRONT_PIECES // FRONT_SLOTS + 1 if half == 0 else 1
                    full = pe.snap(16 * i + 16 * first)
                    full_rest = pe.snap(16 * i + 16)
                    with pe.Fori(0, n) as _c:
                        expert_block(3 * half, full, full_rest)

            turns(0)
            pe.wait_ge(order_ready, 1)
            with pe.Fori(1, EXPERTS // 2) as i:
                turns(i)
            total = pe.snap(blk)
            pe.wait_ge(gm_ready, total)
            pe.wait_ge(res_ready, total)
            combine(True)


_INS = ["x", "c", "w_mod", "b_mod", "g_pre_mix", "g_post_mix", "w_in", "b_in", "attn_sinks",
        "sg_ln_g", "sg_ln_b", "sg_w", "sg_b", "w_br_attn", "w_br_sg", "w_out", "b_out",
        "g_pre_ffn", "g_post_ffn", "w_router", "b_router", "w_mlp1", "b_mlp1", "w_mlp2", "b_mlp2"]


def kernel(**inputs):
    import concourse.bacc as bacc
    from concourse.bass_utils import run_bass_kernel_spmd

    nc = bacc.Bacc("TRN2", target_bir_lowering=False, num_devices=1, dynamic_dma_scratch_size=64)
    arrays, t = {}, {}
    for name in _INS:
        a = np.ascontiguousarray(inputs[name])
        arrays[name] = a
        t[name] = nc.dram_tensor(name, a.shape, F32, kind="ExternalInput").ap()
    arrays["rank_of_turn"] = np.array([RANK_OF_TURN], dtype=np.float32)
    t["rank_of_turn"] = nc.dram_tensor("rank_of_turn", (1, RANKS), F32, kind="ExternalInput").ap()
    out = nc.dram_tensor("out", (1, SEQ, D), F32, kind="ExternalOutput").ap()
    layer_program(nc, t, out)
    r = run_bass_kernel_spmd(nc, [arrays], core_ids=[0])
    return r.results[0]["out"]
```
